# Optimizing a Trainium2 kernel written in Bass

```python
import jax, jax.numpy as jnp
from jax import lax
import numpy as np

D_MODEL = 1024
BATCH = 1
SEQ = 1024
DEPTH = 1

CONV_WIDTH = D_MODEL
CONV_K = 3
N_Q_HEADS = 16
N_KV_HEADS = 2
HEAD_DIM = 64
ATTN_WIDTH = N_Q_HEADS * HEAD_DIM
KV_WIDTH = N_KV_HEADS * HEAD_DIM
GROUP = N_Q_HEADS // N_KV_HEADS
WINDOW = 128
BLOCK = 128
PROJ_WIDTH = 3 * CONV_WIDTH + ATTN_WIDTH + 2 * KV_WIDTH
D_FF = 2816
FFN_RESIDUAL = 0.5
N_BRANCHES = 2
EPS = 1e-6
NEG_INF = -1e30

kernel_name = "hybrid_shortconv_swa_sink_macaron_block"

def rms_norm(x, w):
    xf = x.astype(jnp.float32)
    y = xf * lax.rsqrt(jnp.mean(xf * xf, axis=-1, keepdims=True) + EPS)
    return (y * w.astype(jnp.float32)).astype(x.dtype)

def swiglu(x, w_gate, w_up, w_down):
    return (jax.nn.silu(x @ w_gate) * (x @ w_up)) @ w_down

def causal_depthwise_conv(z, w):
    S = z.shape[1]
    zp = jnp.pad(z, ((0, 0), (CONV_K - 1, 0), (0, 0)))
    y = zp[:, 0:S] * w[0]
    for k in range(1, CONV_K):
        y = y + zp[:, k:k + S] * w[k]
    return y

def sliding_window_attention(q, k, v, sinks):
    B, S = q.shape[0], q.shape[1]
    nb = S // BLOCK
    qb = q.reshape(B, nb, BLOCK, N_KV_HEADS, GROUP, HEAD_DIM)
    pad = jnp.zeros((B, BLOCK, N_KV_HEADS, HEAD_DIM), k.dtype)
    kp = jnp.concatenate([pad, k], axis=1).reshape(B, nb + 1, BLOCK, N_KV_HEADS, HEAD_DIM)
    vp = jnp.concatenate([pad, v], axis=1).reshape(B, nb + 1, BLOCK, N_KV_HEADS, HEAD_DIM)
    kb = jnp.concatenate([kp[:, :-1], kp[:, 1:]], axis=2)
    vb = jnp.concatenate([vp[:, :-1], vp[:, 1:]], axis=2)
    scale = HEAD_DIM ** -0.5
    scores = jnp.einsum('bnqhgd,bnkhd->bnhgqk', qb, kb).astype(jnp.float32) * scale
    qpos = jnp.arange(BLOCK)[:, None] + BLOCK
    kpos = jnp.arange(2 * BLOCK)[None, :]
    band = (kpos <= qpos) & (qpos - kpos < WINDOW)
    not_pad = (jnp.arange(nb)[:, None, None] > 0) | (kpos[None] >= BLOCK)
    mask = band[None] & not_pad
    scores = jnp.where(mask[None, :, None, None], scores, NEG_INF)
    sink = sinks.astype(jnp.float32).reshape(N_KV_HEADS, GROUP)[None, None, :, :, None, None]
    sink = jnp.broadcast_to(sink, scores.shape[:-1] + (1,))
    probs = jax.nn.softmax(jnp.concatenate([scores, sink], axis=-1), axis=-1)[..., :-1]
    out = jnp.einsum('bnhgqk,bnkhd->bnqhgd', probs.astype(v.dtype), vb)
    return out.reshape(B, S, ATTN_WIDTH)

def setup_inputs(seed: int = 0) -> dict:
    key = jax.random.key(seed)
    ks = jax.random.split(key, 24)
    L, D = DEPTH, D_MODEL

    def w(k, shape, fan_in):
        return jax.random.normal(k, shape, jnp.float32) * fan_in ** -0.5

    def gain(k, shape):
        return 1.0 + 0.05 * jax.random.normal(k, shape, jnp.float32)

    return {
        "x": jax.random.normal(ks[0], (BATCH, SEQ, D), jnp.float32),
        "ffn1_norm": gain(ks[1], (L, D)),
        "ffn1_w_gate": w(ks[2], (L, D, D_FF), D),
        "ffn1_w_up": w(ks[3], (L, D, D_FF), D),
        "ffn1_w_down": w(ks[4], (L, D_FF, D), D_FF),
        "mix_norm": gain(ks[5], (L, D)),
        "w_in": w(ks[6], (L, D, PROJ_WIDTH), D),
        "conv_w": w(ks[7], (L, CONV_K, CONV_WIDTH), CONV_K),
        "q_norm": gain(ks[8], (L, HEAD_DIM)),
        "k_norm": gain(ks[9], (L, HEAD_DIM)),
        "sinks": 0.5 * jax.random.normal(ks[10], (L, N_Q_HEADS), jnp.float32),
        "w_conv_out": w(ks[11], (L, CONV_WIDTH, D), CONV_WIDTH),
        "w_attn_out": w(ks[12], (L, ATTN_WIDTH, D), ATTN_WIDTH),
        "w_branch_gate": w(ks[13], (L, D, N_BRANCHES * D), D),
        "b_branch_gate": 0.02 * jax.random.normal(ks[14], (L, N_BRANCHES * D), jnp.float32),
        "w_out": w(ks[15], (L, D, D), D),
        "ffn2_norm": gain(ks[16], (L, D)),
        "ffn2_w_gate": w(ks[17], (L, D, D_FF), D),
        "ffn2_w_up": w(ks[18], (L, D, D_FF), D),
        "ffn2_w_down": w(ks[19], (L, D_FF, D), D_FF),
    }

def reference(x, ffn1_norm, ffn1_w_gate, ffn1_w_up, ffn1_w_down, mix_norm, w_in, conv_w,
              q_norm, k_norm, sinks, w_conv_out, w_attn_out, w_branch_gate, b_branch_gate,
              w_out, ffn2_norm, ffn2_w_gate, ffn2_w_up, ffn2_w_down):
    B, S = x.shape[0], x.shape[1]
    for l in range(DEPTH):
        x = x + FFN_RESIDUAL * swiglu(rms_norm(x, ffn1_norm[l]), ffn1_w_gate[l], ffn1_w_up[l], ffn1_w_down[l])

        h = rms_norm(x, mix_norm[l])
        p = h @ w_in[l]
        c0 = 3 * CONV_WIDTH
        gb, gc, vc = jnp.split(p[..., :c0], 3, axis=-1)
        q = p[..., c0:c0 + ATTN_WIDTH].reshape(B, S, N_Q_HEADS, HEAD_DIM)
        k = p[..., c0 + ATTN_WIDTH:c0 + ATTN_WIDTH + KV_WIDTH].reshape(B, S, N_KV_HEADS, HEAD_DIM)
        v = p[..., c0 + ATTN_WIDTH + KV_WIDTH:].reshape(B, S, N_KV_HEADS, HEAD_DIM)

        y_conv = (gb * causal_depthwise_conv(gc * vc, conv_w[l])) @ w_conv_out[l]

        q = rms_norm(q, q_norm[l])
        k = rms_norm(k, k_norm[l])
        y_attn = sliding_window_attention(q, k, v, sinks[l]) @ w_attn_out[l]

        g = jax.nn.sigmoid(h @ w_branch_gate[l] + b_branch_gate[l]).reshape(B, S, N_BRANCHES, D_MODEL)
        merged = g[:, :, 0] * y_conv + g[:, :, 1] * y_attn
        x = x + merged @ w_out[l]

        x = x + FFN_RESIDUAL * swiglu(rms_norm(x, ffn2_norm[l]), ffn2_w_gate[l], ffn2_w_up[l], ffn2_w_down[l])
    return x


_drawn_inputs = setup_inputs


def setup_inputs(seed=0):
    import zlib

    import numpy as np

    out = dict(_drawn_inputs(seed))
    spreads = {}
    factors = {'q_norm': 8.0, 'k_norm': 8.0, 'sinks': 200.0, 'b_branch_gate': 8.0, 'ffn2_norm': 3.235}
    for name, (base, spread) in spreads.items():
        noise = np.random.default_rng([zlib.crc32(name.encode()), seed]).standard_normal(out[name].shape)
        drawn = base * np.exp(spread * noise) if base else spread * noise
        out[name] = __import__('jax').numpy.asarray(drawn.astype(out[name].dtype))
    for name, factor in factors.items():
        out[name] = (out[name] * factor).astype(out[name].dtype)
    return out
```

```python
from contextlib import ExitStack

import concourse.bass as bass
from concourse import mybir

F32 = mybir.dt.float32
F32R = mybir.dt.float32r
ALU = mybir.AluOpType
ACT = mybir.ActivationFunctionType
AX_X = mybir.AxisListType.X

P = 128
T = 512
SLAB = 4
RING = 4
EPS = 1e-6
NEG = -1e30
C_MASK, C_IDENT, C_ONES, C_HALVES, C_SEL, C_END = 0, 384, 512, 640, 768, 770


class Shapes:

    def __init__(s, D, S, F, heads, kv_heads, hd):
        s.D, s.S, s.F, s.hd = D, S, F, hd
        s.DT, s.FT, s.CH = D // P, F // P, S // T
        s.QT = heads * hd // P
        s.BLK = T // P
        s.DS = s.DT // SLAB
        s.FS = -(-s.FT // SLAB)
        assert kv_heads == 2 and 2 * hd == P and s.DT == s.QT == 8 and s.FT % 2 == 0
        up, down = (s.FT * 2 * s.DS, s.FT * 2), (s.DT * s.FS, s.DT)
        sizes = [("up0", up), ("down0", down), ("kv", (2 * s.DS, 2)), ("q", (s.QT * s.DS, s.QT)),
                 ("conv", (3 * s.DT * s.DS, 3 * s.DT)), ("merge", (4 * s.DT * s.DS, 4 * s.DT)),
                 ("out", (s.DT * s.DS, s.DT)), ("up1", up), ("down1", down)]
        s.slab_at, s.panel_at, s.slabs, s.panels = {}, {}, 0, 0
        for name, (ns, np_) in sizes:
            s.slab_at[name], s.panel_at[name] = s.slabs, s.panels
            s.slabs, s.panels = s.slabs + ns, s.panels + np_
        assert s.slabs % RING == 0
        assert all(v % RING == 0 for v in s.slab_at.values())


def block_program(nc, sh, x, slabs, consts, vectors, out):
    DT, FT, QT, DS, FS, CH, BLK = sh.DT, sh.FT, sh.QT, sh.DS, sh.FS, sh.CH, sh.BLK
    W = SLAB * P
    GROUPS = 4 * BLK
    KVR = BLK + 1
    V_NORM, V_CONV, V_BIAS, V_SINK, V_QN, V_KN = 0, 3 * DT, 6 * DT, 8 * DT, 8 * DT + 16, 8 * DT + 17
    SCALE = float(sh.hd) ** -0.5

    with ExitStack() as ctx:
        def sb(name, shape, dt=F32):
            return ctx.enter_context(nc.sbuf_tensor(name, shape, dt))

        def sem(name):
            return ctx.enter_context(nc.semaphore(name))

        bank = ctx.enter_context(nc.psum_tensor("bank", [P, 8, T], F32))
        SCORES, TRANS, STAT = 4, 6, 7

        raw = sb("raw", [P, RING, W])
        w_hi = sb("w_hi", [P, RING, W], F32R)
        w_lo = sb("w_lo", [P, RING, W], F32R)
        res = sb("res", [P, DT, T])
        h_hi = sb("h_hi", [P, DT, T], F32R)
        h_lo = sb("h_lo", [P, DT, T], F32R)
        G = max(FT, 3 * DT)
        g_hi = sb("g_hi", [P, G, T], F32R)
        g_lo = sb("g_lo", [P, G, T], F32R)
        Y0, Q0, M0 = 0, DT, 2 * DT
        k_hi = sb("k_hi", [P, KVR, P], F32R)
        k_lo = sb("k_lo", [P, KVR, P], F32R)
        v_hi = sb("v_hi", [P, KVR, 3 * sh.hd], F32R)
        v_lo = sb("v_lo", [P, KVR, 3 * sh.hd], F32R)
        tmp = sb("tmp", [P, 4 * T + 8])
        sq = sb("sq", [P, 2, T])
        nt = sb("nt", [P, 3, T])
        rs = sb("rs", [P, T])
        rs2 = sb("rs2", [P, T])
        cst = sb("cst", [P, C_END])
        vec = sb("vec", [P, vectors.shape[1]])
        carry = sb("carry", [P, DT, 2])
        rq = sb("rq", [P, 2 * QT * BLK])
        mx = sb("mx", [P, 2, 4])
        shift = sb("shift", [P, 2, 4])
        esink = sb("esink", [P, 2, 4])
        den = sb("den", [P, 2, 4])

        def t_(j):
            return tmp[:, j * T:(j + 1) * T]

        z = tmp[:, 3 * T:4 * T + 2]
        ssq, var, root = nt[:, 0, :], nt[:, 1, :], nt[:, 2, :]
        sm = [sq[:, :, :].rearrange("p a b -> p (a b)"),
              nt[:, 0:2, :].rearrange("p a b -> p (a b)")]
        ident, ones = cst[:, C_IDENT:C_IDENT + P], cst[:, C_ONES:C_ONES + P]
        halves, sel = cst[:, C_HALVES:C_HALVES + P], cst[:, C_SEL:C_SEL + 2]

        raw_landed = [sem(f"raw_landed{j}") for j in range(RING)]
        w_hi_ready = sem("w_hi_ready")
        w_lo_ready = sem("w_lo_ready")
        multiplied = sem("multiplied")
        panel_read = sem("panel_read")
        const_landed = sem("const_landed")
        zeroed = sem("zeroed")
        x_loaded = [sem(f"x_loaded{j}") for j in range(4)]
        stored = [sem(f"stored{j}") for j in range(4)]
        prep_hi = sem("prep_hi")
        ssq_added = sem("ssq_added")
        h_ready = sem("h_ready")
        stat_done = sem("stat_done")
        var_ready = sem("var_ready")
        root_ready = sem("root_ready")
        silu_done = sem("silu_done")
        product = sem("product")
        hid_hi = sem("hid_hi")
        hid_ready = sem("hid_ready")
        k_squared = sem("k_squared")
        v_turned = sem("v_turned")
        k_scaled = sem("k_scaled")
        kv_hi = sem("kv_hi")
        kv_ready = sem("kv_ready")
        q_hi = sem("q_hi")
        q_ready = sem("q_ready")
        q_summed = sem("q_summed")
        rq_ready = sem("rq_ready")
        scored = sem("scored")
        scores_read = sem("scores_read")
        shifted = sem("shifted")
        exps_done = sem("exps_done")
        probs_ready = sem("probs_ready")
        turned = sem("turned")
        turned_hi = sem("turned_hi")
        turned_ready = sem("turned_ready")
        weighed = sem("weighed")
        o_hi = sem("o_hi")
        o_ready = sem("o_ready")
        conv_sum = sem("conv_sum")
        y_hi = sem("y_hi")
        y_ready = sem("y_ready")
        gate_done = sem("gate_done")
        merged = sem("merged")
        merged_hi = sem("merged_hi")
        merged_ready = sem("merged_ready")
        dve_step = sem("dve_step")
        up_scaled = sem("up_scaled")

        def wait(eng, s, value):
            if not isinstance(value, int) or value > 0:
                eng.wait_ge(s, value)

        def slab0(c, phase):
            return c * sh.slabs + sh.slab_at[phase]

        def panel0(c, phase):
            return c * sh.panels + sh.panel_at[phase]

        def prep0(c, stage):
            return (3 * c + stage) * DT

        def group(c, s):
            kv, g, n = s % 2, s // 2 % 2, s // 4
            b = c * BLK + n
            now, before = (b + 1) % KVR, b % KVR
            if b == 0:
                return g, kv, n, [now], P
            return g, kv, n, ([before, now] if before < now else [now, before]), (0 if before < now else P)

        def turns_before(c, s):
            return 2 * (c * GROUPS + s) - min(4, c * GROUPS + s)

        def body_values(i, per):
            return i * per

        block = ctx.enter_context(nc.Block())

        @block.sync
        def _(sp):
            sp.dma_start(cst[:, :], consts).then_inc(const_landed, 16)
            sp.dma_start(vec[:, :], vectors).then_inc(const_landed, 16)
            for c in range(CH):
                first = 1 if c == 0 else 0
                if c == 0:
                    for j in range(RING):
                        sp.dma_start(raw[:, j, :], slabs[j]).then_inc(raw_landed[j], 16)
                with sp.Fori(first, sh.slabs // RING) as i:
                    for j in range(RING):
                        sp.wait_ge(w_lo_ready, c * sh.slabs + j + 1 - RING + i * RING)
                        sp.dma_start(raw[:, j, :], slabs[i * RING + j]).then_inc(raw_landed[j], 16)

        @block.gpsimd
        def _(pool):
            with pool.Fori(0, CH * sh.slabs // RING) as i:
                for j in range(RING):
                    pool.wait_ge(w_hi_ready, i * RING + (j + 1))
                    nc.gpsimd.tensor_tensor(w_lo[:, j, :], raw[:, j, :], w_hi[:, j, :].bitcast(F32),
                                            ALU.subtract).then_inc(w_lo_ready, 1)

        @block.tensor
        def _(pe):
            def products(n0, off, nk, b, rhs, start, stop, ready=None):
                j = n0 % RING
                wait(pe, w_hi_ready, n0 + 1 + off)
                for k in range(nk):
                    if ready:
                        pe.wait_ge(*ready(k))
                    hi, lo = rhs(k)
                    wt = w_hi[:, j, k * P:(k + 1) * P]
                    pe.matmul(bank[:, b, :], wt, hi, start=start and k == 0, stop=False)
                    pe.matmul(bank[:, b, :], wt, lo, start=False, stop=False)
                wait(pe, w_lo_ready, n0 + 1 + off)
                for k in range(nk):
                    last = pe.matmul(bank[:, b, :], w_lo[:, j, k * P:(k + 1) * P], rhs(k)[0],
                                     start=False, stop=stop and k == nk - 1)
                last.then_inc(multiplied, 1)

            def panel(n0, noff, p0, poff, tiles, hi, lo, t0=0, ready=None, gaps=None):
                wait(pe, panel_read, p0 + 1 - 4 + poff)
                ns = -(-tiles // SLAB)
                for s in range(ns):
                    nk = min(SLAB, tiles - s * SLAB)
                    products(n0 + s, noff, nk, p0 % 4,
                             lambda k, s=s: (hi[:, t0 + s * SLAB + k, :], lo[:, t0 + s * SLAB + k, :]),
                             s == 0, s == ns - 1,
                             ready and (lambda k, s=s: ready(s * SLAB + k)))
                    if gaps:
                        gaps(s)

            def sum_squares(e, free=None):
                pe.matmul(bank[:, STAT, :], ones, ssq, start=True, stop=True).then_inc(stat_done, 1)

            def ffn(c, w):
                n, p = slab0(c, f"up{w}"), panel0(c, f"up{w}")
                r = prep0(c, 2 * w)

                def body(f0, off):
                    for j in range(4):
                        first = f0 == 0 and j == 0
                        panel(n + (2 * f0 + j) * DS, 2 * DS * off, p + 2 * f0 + j, 2 * off, DT, h_hi, h_lo,
                              ready=(lambda k: (h_ready, r + k + 1)) if first else None)
                        if first:
                            sum_squares(0)

                body(0, 0)
                with pe.Fori(0, FT // 2 - 1) as i:
                    body(2, i * 2)
                residual(c, f"down{w}", FT, g_hi, g_lo, 0, hid_ready, (2 * c + w) * FT)

            def residual(c, phase, tiles, hi, lo, t0, sem_, base):
                ns = -(-tiles // SLAB)
                n, p = slab0(c, phase), panel0(c, phase)
                with pe.Fori(0, DT // 4) as i:
                    for j in range(4):
                        panel(n + j * ns, i * (4 * ns), p + j, i * 4, tiles, hi, lo, t0,
                              ready=(lambda k: (sem_, base + k + 1)) if j == 0 else None)

            def q_sum(c, t):
                pe.wait_ge(q_hi, c * QT + t + 1)
                if t == 0:
                    pe.wait_ge(var_ready, 5 * c + 3)
                for b in range(BLK):
                    col = b * 2 * QT + 2 * t
                    last = pe.matmul(bank[:, STAT, col:col + 2], sq[:, t % 2, b * P:(b + 1) * P], sel,
                                     start=True, stop=True)
                last.then_inc(q_summed, 1)

            def scores(c, s):
                g, kv, n, pos, _ = group(c, s)
                a, rows, nb = c * GROUPS + s, slice(64 * kv, 64 * kv + 64), len(pos)
                wait(pe, scores_read, a)
                if s == 0:
                    pe.wait_ge(kv_ready, 2 * c + 2)
                    pe.wait_ge(q_ready, (c + 1) * QT)
                step = pos[-1] - pos[0] or 1
                ks = slice(pos[0], pos[-1] + 1, step)
                for h in range(4):
                    o = bank[:, SCORES + h // 2, h % 2 * 2 * P:(h % 2 * 2 + nb) * P]
                    qt = [q[rows, Q0 + 4 * g + h, n * P:(n + 1) * P] for q in (g_hi, g_lo)]
                    kt = [k[rows, ks, :] for k in (k_hi, k_lo)]
                    pe.matmul(o, qt[0], kt[0], start=True, stop=False)
                    pe.matmul(o, qt[0], kt[1], start=False, stop=False)
                    last = pe.matmul(o, qt[1], kt[0], start=False, stop=True)
                last.then_inc(scored, 1)

            def turn(c, s, w):
                a, at = c * GROUPS + s, turns_before(c, s) + w
                pe.wait_ge(probs_ready, a + 1)
                if at:
                    pe.wait_ge(turned_ready, at)
                else:
                    pe.wait_ge(kv_ready, 1)
                for h in range(4):
                    last = pe.transpose(bank[:, TRANS, h * P:(h + 1) * P],
                                        sm[s % 2][:, (2 * h + w) * P:(2 * h + w + 1) * P], ident)
                last.then_inc(turned, 1)

            def weigh(c, s):
                g, kv, n, pos, _ = group(c, s)
                pair = (c * GROUPS + s) // 2
                pe.wait_ge(turned_ready, turns_before(c, s) + len(pos))
                if kv == 0:
                    wait(pe, o_ready, pair)
                    if s == 0:
                        pe.wait_ge(var_ready, 5 * c + 4)
                cols = slice(64 * kv, 64 * kv + P)
                for w, at in enumerate(pos):
                    first, final = kv == 0 and w == 0, kv == 1 and w == len(pos) - 1
                    vh, vl = v_hi[:, at, cols], v_lo[:, at, cols]
                    ph, pl = g_hi[:, M0 + w, :], g_lo[:, M0 + w, :]
                    pe.matmul(bank[:, STAT, :], vh, ph, start=first, stop=False)
                    pe.matmul(bank[:, STAT, :], vh, pl, start=False, stop=False)
                    last = pe.matmul(bank[:, STAT, :], vl, ph, start=False, stop=final)
                last.then_inc(weighed, 1)

            def attention_gap(c, s):
                k, part = s // 3, s % 3
                if part == 0 and k < GROUPS:
                    scores(c, k)
                if k == 0 or k > GROUPS:
                    return
                nb = len(group(c, k - 1)[3])
                if part == 0 and nb == 2:
                    turn(c, k - 1, 0)
                if part == 1:
                    turn(c, k - 1, nb - 1)
                if part == 2:
                    weigh(c, k - 1)

            def mixer(c):
                r = prep0(c, 1)
                n, p = slab0(c, "kv"), panel0(c, "kv")
                panel(n, 0, p, 0, DT, h_hi, h_lo, ready=lambda k: (h_ready, r + k + 1))
                sum_squares(1)
                panel(n + DS, 0, p + 1, 0, DT, h_hi, h_lo)
                n, p = slab0(c, "q"), panel0(c, "q")
                for t in range(QT):
                    panel(n + t * DS, 0, p + t, 0, DT, h_hi, h_lo)
                    if t == 1:
                        wait(pe, kv_ready, 2 * c)
                        if c:
                            pe.wait_ge(turned_ready, turns_before(c, 0))
                        pe.wait_ge(panel_read, panel0(c, "kv") + 2)
                        for b in range(BLK):
                            last = pe.transpose(bank[:, TRANS, b * P:(b + 1) * P],
                                                tmp[:, T + b * P:T + (b + 1) * P], ident)
                        last.then_inc(v_turned, 1)
                        pe.wait_ge(k_squared, c + 1)
                        pe.matmul(bank[:, STAT, :], halves, sq[:, 0, :], start=True, stop=True)\
                          .then_inc(stat_done, 1)
                    if t >= 2:
                        q_sum(c, t - 2)
                n, p = slab0(c, "conv"), panel0(c, "conv")
                for j in range(3 * DT):
                    def gaps(s, j=j):
                        if j == 0:
                            q_sum(c, QT - 2 + s)
                        attention_gap(c, 2 * j + s)
                    panel(n + j * DS, 0, p + j, 0, DT, h_hi, h_lo, gaps=gaps)
                n, p = slab0(c, "merge"), panel0(c, "merge")

                def merge(m0, off, tail=False):
                    for j, (hi, lo, t0) in enumerate([(h_hi, h_lo, 0), (h_hi, h_lo, 0),
                                                      (g_hi, g_lo, Y0), (g_hi, g_lo, Q0)]):
                        if tail and j == 2:
                            pe.wait_ge(y_ready, (c + 1) * DT)
                        if tail and j == 3:
                            pe.wait_ge(o_ready, (c + 1) * GROUPS // 2)
                        panel(n + (4 * m0 + j) * DS, off * (4 * DS), p + 4 * m0 + j, off * 4, DT, hi, lo, t0,
                              gaps=(lambda s, j=j: attention_gap(c, 6 * DT + 2 * j + s)) if tail and j < 2
                              else None)

                merge(0, 0, tail=True)
                with pe.Fori(0, DT - 1) as i:
                    merge(1, i)
                residual(c, "out", DT, g_hi, g_lo, M0, merged_ready, c * DT)

            pe.wait_ge(const_landed, 32)
            for c in range(CH):
                ffn(c, 0)
                mixer(c)
                ffn(c, 1)

        @block.scalar
        def _(act):
            total = CH * sh.slabs

            def split(n0, off, final=False):
                j = n0 % RING
                if n0 >= total and final:
                    return
                wait(act, multiplied, n0 + 1 - RING + off)
                act.wait_ge(raw_landed[j], 16 * (n0 // RING + 1) + off * (16 // RING))
                nc.scalar.activation(w_hi[:, j, :], raw[:, j, :], ACT.Copy).then_inc(w_hi_ready, 1)

            def prep(c, stage, m0, off, j):
                r = prep0(c, stage) + m0
                wait(act, ssq_added, r - 1 + off)
                m = off + m0
                nc.scalar.activation(sq[:, j % 2, :], res[:, m, :], ACT.Square)
                nc.scalar.activation(h_hi[:, m, :], res[:, m, :], ACT.Copy,
                                     scale=vec[:, bass.ds(V_NORM + stage * DT + m, 1)])\
                  .then_inc(prep_hi, 1)

            def square_root(e):
                act.wait_ge(var_ready, e + 1)
                if e % 5 == 3:
                    nc.scalar.activation(root[:, 0:2 * QT * BLK], var[:, 0:2 * QT * BLK], ACT.Sqrt)\
                      .then_inc(root_ready, 1)
                else:
                    nc.scalar.activation(root, var, ACT.Sqrt).then_inc(root_ready, 1)

            def load_x(c, m0, off, j):
                act.dma_start(res[:, off + m0, :], x[c, off + m0]).then_inc(x_loaded[j], 16)

            def ffn(c, w):
                n, p, fb = slab0(c, f"up{w}"), panel0(c, f"up{w}"), (2 * c + w) * FT
                ahead = RING - 1

                def body(f0, off):
                    for j in range(2):
                        f = f0 + j
                        for s in range(DS):
                            split(n + 2 * f * DS + s + ahead, off * (2 * DS))
                        if f == 0:
                            square_root(5 * c + 4 * w)
                        act.wait_ge(panel_read, p + 2 * f + 1 + off * 2)
                        nc.scalar.activation(t_(j), t_(j), ACT.Silu).then_inc(silu_done, 1)
                        for s in range(DS):
                            split(n + (2 * f + 1) * DS + s + ahead, off * (2 * DS))
                        act.wait_ge(product, fb + f + 1 + off)
                        nc.scalar.activation(g_hi[:, off + f, :], t_(2 + j), ACT.Copy).then_inc(hid_hi, 1)

                body(0, 0)
                with act.Fori(0, FT // 2 - 1) as i:
                    body(2, i * 2)
                if w == 0:
                    residual(c, "down0", FS, 1)
                else:
                    output(c)

            def residual(c, phase, ns, stage):
                n, p = slab0(c, phase), panel0(c, phase)
                with act.Fori(0, DT // 4) as i:
                    for j in range(4):
                        for s in range(ns):
                            split(n + j * ns + s + RING - 1, i * (4 * ns))
                        act.wait_ge(panel_read, p + j + 1 + i * 4)
                        prep(c, stage, j, i * 4, j)

            def output(c):
                n, p = slab0(c, "down1"), panel0(c, "down1")
                more = c + 1 < CH

                def body(m0, off, final):
                    for j in range(4):
                        for s in range(FS):
                            split(n + (m0 + j) * FS + s + RING - 1, off * FS, final)
                        act.wait_ge(panel_read, p + m0 + j + 1 + off)
                        act.dma_start(out[c, off + m0 + j], t_(j)).then_inc(stored[j], 16)
                        if more:
                            load_x(c + 1, m0 + j, off, j)
                            if m0 + j:
                                m, q = m0 + j - 1, (j - 1) % 4
                                act.wait_ge(x_loaded[q], 16 * ((c + 1) * DT // 4 + m // 4 + 1))
                                prep(c + 1, 0, m, off, q)

                for m0 in range(0, DT, 4):
                    body(m0, 0, True)
                if more:
                    act.wait_ge(x_loaded[3], 16 * (c + 2) * DT // 4)
                    prep(c + 1, 0, DT - 1, 0, 3)

            def exps(c, s):
                g, kv, n, pos, _ = group(c, s)
                act.wait_ge(shifted, c * GROUPS + s + 1)
                for h in range(4):
                    v = sm[kv][:, 2 * h * P:(2 * h + len(pos)) * P]
                    nc.scalar.activation(v, v, ACT.Exp, bias=shift[:, kv, h:h + 1],
                                         accum_out=den[:, kv, h:h + 1])
                nc.scalar.activation(esink[:, kv, :], esink[:, kv, :], ACT.Exp).then_inc(exps_done, 1)

            def turn_hi(c, s, w):
                act.wait_ge(turned, turns_before(c, s) + w + 1)
                nc.scalar.activation(g_hi[:, M0 + w, :], bank[:, TRANS, :], ACT.Copy).then_inc(turned_hi, 1)

            def weigh_hi(c, s):
                if s % 2:
                    g, kv, n, _, _ = group(c, s)
                    act.wait_ge(weighed, c * GROUPS + s + 1)
                    nc.scalar.activation(g_hi[:, Q0 + 4 * g:Q0 + 4 * g + 4, n * P:(n + 1) * P],
                                         bank[:, STAT, :].rearrange("p (h q) -> p h q", h=4), ACT.Copy)\
                      .then_inc(o_hi, 1)

            def conv_hi(c, m):
                act.wait_ge(conv_sum, c * DT + m + 1)
                nc.scalar.activation(g_hi[:, Y0 + m, :], t_(2), ACT.Copy).then_inc(y_hi, 1)

            def attention_gap(c, s):
                k, part = s // 3, s % 3
                if k > GROUPS:
                    return
                nb = len(group(c, k - 1)[3]) if k else 0
                if part == 0 and nb == 2:
                    turn_hi(c, k - 1, 0)
                if part == 0 and k < GROUPS:
                    exps(c, k)
                if part == 1 and k:
                    turn_hi(c, k - 1, nb - 1)
                if part == 2 and k:
                    weigh_hi(c, k - 1)

            def mixer(c):
                n, p = slab0(c, "kv"), panel0(c, "kv")
                for s in range(DS):
                    split(n + s + RING - 1, 0)
                square_root(5 * c + 1)
                for s in range(DS):
                    split(n + DS + s + RING - 1, 0)
                act.wait_ge(panel_read, p + 1)
                nc.scalar.activation(sq[:, 0, :], t_(0), ACT.Square).then_inc(k_squared, 1)
                n, p = slab0(c, "q"), panel0(c, "q")
                for t in range(QT):
                    for s in range(DS):
                        split(n + t * DS + s + RING - 1, 0)
                    if t == 0:
                        act.wait_ge(stat_done, 4 * c + 3)
                    act.wait_ge(panel_read, p + t + 1)
                    if t >= 2:
                        act.wait_ge(q_summed, c * QT + t - 1)
                    nc.scalar.activation(sq[:, t % 2, :], t_(2 + t % 2), ACT.Square)
                    nc.scalar.activation(g_hi[:, Q0 + t, :], t_(2 + t % 2), ACT.Copy,
                                         scale=vec[:, V_QN:V_QN + 1]).then_inc(q_hi, 1)
                    if t == 0:
                        act.wait_ge(v_turned, c + 1)
                        at = [(c * BLK + b + 1) % KVR for b in range(BLK)]
                        assert at == list(range(at[0], at[0] + BLK))
                        nc.scalar.activation(
                            v_hi[:, at[0]:at[0] + BLK, :].rearrange("p b (k d) -> p b k d", k=3)[:, :, 0::2, :],
                            bank[:, TRANS, :].rearrange("p (b k d) -> p b k d", b=BLK, k=2), ACT.Copy)\
                          .then_inc(kv_hi, 1)
                        square_root(5 * c + 2)
                        act.wait_ge(k_scaled, c + 1)
                        nc.scalar.activation(k_hi[:, at[0]:at[0] + BLK, :],
                                             t_(0).rearrange("p (b d) -> p b d", b=BLK), ACT.Copy,
                                             scale=vec[:, V_KN:V_KN + 1]).then_inc(kv_hi, 1)
                n = slab0(c, "conv")
                for s in range(3 * DT * DS):
                    split(n + s + RING - 1, 0)
                    if s == 0:
                        square_root(5 * c + 3)
                    if s and s % 6 == 0:
                        conv_hi(c, s // 6 - 1)
                    attention_gap(c, s)
                conv_hi(c, DT - 1)
                n, p = slab0(c, "merge"), panel0(c, "merge")

                def merge(m0, off, tail=False):
                    for j in range(4):
                        for s in range(DS):
                            split(n + (4 * m0 + j) * DS + s + RING - 1, off * (4 * DS))
                            if tail and j < 2:
                                attention_gap(c, 6 * DT + 2 * j + s)
                        if j < 2:
                            act.wait_ge(panel_read, p + 4 * m0 + j + 1 + off * 4)
                            nc.scalar.activation(t_(j), t_(j), ACT.Sigmoid,
                                                 bias=vec[:, bass.ds(V_BIAS + j * DT + m0 + off, 1)])\
                              .then_inc(gate_done, 1)
                    act.wait_ge(merged, c * DT + m0 + 1 + off)
                    nc.scalar.activation(g_hi[:, off + (M0 + m0), :], t_(2), ACT.Copy).then_inc(merged_hi, 1)

                merge(0, 0, tail=True)
                with act.Fori(0, DT - 1) as i:
                    merge(1, i)
                residual(c, "out", DS, 2)

            for m in range(DT):
                load_x(0, m, 0, m % 4)
            for n in range(RING - 1):
                split(n, 0)
            act.wait_ge(const_landed, 32)
            for m in range(DT):
                act.wait_ge(x_loaded[m % 4], 16 * DT // 4)
                prep(0, 0, m, 0, m % 4)
            for c in range(CH):
                ffn(c, 0)
                mixer(c)
                ffn(c, 1)
            for j in range(4):
                act.wait_ge(stored[j], 16 * CH * DT // 4)

        @block.vector
        def _(dve):
            steps = [0]

            def settle(ins):
                steps[0] += 1
                ins.then_inc(dve_step, 1)
                dve.wait_ge(dve_step, steps[0])

            def prep(c, stage, m0, off, j):
                r, m = prep0(c, stage) + m0, off + m0
                dve.wait_ge(prep_hi, r + 1 + off)
                if m0 == 0 and isinstance(off, int):
                    nc.vector.tensor_copy(ssq, sq[:, j % 2, :]).then_inc(ssq_added, 1)
                else:
                    wait(dve, ssq_added, r + off)
                    nc.vector.tensor_tensor(ssq, ssq, sq[:, j % 2, :], ALU.add).then_inc(ssq_added, 1)
                nc.vector.scalar_tensor_tensor(
                    out=h_lo[:, m, :], in0=res[:, m, :], scalar=vec[:, bass.ds(V_NORM + stage * DT + m, 1)],
                    in1=h_hi[:, m, :].bitcast(F32), op0=ALU.mult, op1=ALU.subtract).then_inc(h_ready, 1)

            def rsqrt(e, dst, count, cols=T, scale=None):
                v, r, y = var[:, 0:cols], root[:, 0:cols], nt[:, 0, 0:cols]
                nc.vector.tensor_scalar(v, bank[:, STAT, 0:cols], 1.0 / count, EPS, ALU.mult, ALU.add)\
                  .then_inc(var_ready, 1)
                dve.wait_ge(root_ready, e + 1)
                settle(nc.vector.reciprocal(y, r))
                settle(nc.vector.tensor_tensor(r, y, y, ALU.mult))
                settle(nc.vector.tensor_tensor(r, r, v, ALU.mult))
                settle(nc.vector.tensor_scalar(r, r, -0.5, 1.5, ALU.mult, ALU.add))
                if scale:
                    settle(nc.vector.tensor_scalar(r, r, scale, None, ALU.mult))
                settle(nc.vector.tensor_tensor(dst, y, r, ALU.mult))

            def scaled(n, noff, p0, dst, poff=0):
                dve.wait_ge(multiplied, n + noff)
                return nc.vector.tensor_tensor(dst, bank[:, p0 % 4, :], rs[:, :], ALU.mult)\
                    .then_inc(panel_read, 1)

            def hidden_lo(fb, f0, off, j):
                dve.wait_ge(hid_hi, fb + f0 + 1 + off)
                nc.vector.tensor_tensor(g_lo[:, off + f0, :], t_(2 + j), g_hi[:, off + f0, :].bitcast(F32),
                                        ALU.subtract).then_inc(hid_ready, 1)

            def ffn(c, w):
                n, p, fb = slab0(c, f"up{w}"), panel0(c, f"up{w}"), (2 * c + w) * FT
                dve.wait_ge(stat_done, 4 * c + (1 if w == 0 else 4))
                rsqrt(5 * c + 4 * w, rs[:, :], sh.D)

                def body(f0, off):
                    for j in range(2):
                        f = f0 + j
                        scaled(n + (2 * f + 1) * DS, off * (2 * DS), p + 2 * f, t_(j))
                        if f:
                            hidden_lo(fb, f - 1, off, 1 - j)
                        scaled(n + (2 * f + 2) * DS, off * (2 * DS), p + 2 * f + 1, t_(2 + j))
                        dve.wait_ge(silu_done, fb + f + 1 + off)
                        dve.wait_ge(panel_read, p + 2 * f + 2 + off * 2)
                        nc.vector.tensor_tensor(t_(2 + j), t_(j), t_(2 + j), ALU.mult).then_inc(product, 1)

                body(0, 0)
                with dve.Fori(0, FT // 2 - 1) as i:
                    body(2, i * 2)
                hidden_lo(fb, FT - 1, 0, 1)
                if w == 0:
                    residual(c, "down0", FS, 1, 0.5)
                else:
                    output(c)

            def residual(c, phase, ns, stage, factor):
                n, p = slab0(c, phase), panel0(c, phase)

                def body(m0, off, first=False):
                    for j in range(4):
                        dve.wait_ge(multiplied, n + (m0 + j + 1) * ns + off * ns)
                        m = off + (m0 + j)
                        nc.vector.scalar_tensor_tensor(out=res[:, m, :], in0=bank[:, (p + j) % 4, :],
                                                       scalar=factor, in1=res[:, m, :], op0=ALU.mult,
                                                       op1=ALU.add).then_inc(panel_read, 1)
                        if m0 + j:
                            prep(c, stage, m0 + j - 1, off, (j - 1) % 4)

                body(0, 0)
                with dve.Fori(0, DT // 4 - 1) as i:
                    body(4, i * 4)
                prep(c, stage, DT - 1, 0, 3)

            def output(c):
                n, p = slab0(c, "down1"), panel0(c, "down1")
                more = c + 1 < CH
                for m in range(DT):
                    dve.wait_ge(multiplied, n + (m + 1) * FS)
                    wait(dve, stored[m % 4], 16 * (c * DT // 4 + m // 4))
                    nc.vector.scalar_tensor_tensor(out=t_(m % 4), in0=bank[:, (p + m) % 4, :], scalar=0.5,
                                                   in1=res[:, m, :], op0=ALU.mult, op1=ALU.add)\
                      .then_inc(panel_read, 1)
                    if more and m:
                        prep(c + 1, 0, m - 1, 0, (m - 1) % 4)
                if more:
                    prep(c + 1, 0, DT - 1, 0, 3)
                    for j in range(4):
                        dve.wait_ge(stored[j], 16 * (c + 1) * DT // 4)

            def mask_and_max(c, s):
                g, kv, n, pos, mask = group(c, s)
                nb = len(pos)
                dve.wait_ge(scored, c * GROUPS + s + 1)
                for h in range(4):
                    col = n * 2 * QT + 2 * (4 * g + h) + kv
                    last = nc.vector.scalar_tensor_tensor(
                        out=sm[kv][:, 2 * h * P:(2 * h + nb) * P],
                        in0=bank[:, SCORES + h // 2, h % 2 * 2 * P:(h % 2 * 2 + nb) * P],
                        scalar=rq[:, col:col + 1], in1=cst[:, C_MASK + mask:C_MASK + mask + nb * P],
                        op0=ALU.mult, op1=ALU.add)
                last.then_inc(scores_read, 1)
                dve.wait_ge(scores_read, c * GROUPS + s + 1)
                sink = vec[:, V_SINK + kv * QT + 4 * g:V_SINK + kv * QT + 4 * g + 4]
                v = sm[kv].rearrange("p (h k) -> p h k", h=4)[:, :, 0:nb * P]
                settle(nc.vector.tensor_reduce(mx[:, kv, :], v, AX_X, ALU.max))
                settle(nc.vector.tensor_tensor(mx[:, kv, :], mx[:, kv, :], sink, ALU.max))
                nc.vector.tensor_scalar(shift[:, kv, :], mx[:, kv, :], -1.0, None, ALU.mult)
                nc.vector.tensor_tensor(esink[:, kv, :], sink, mx[:, kv, :], ALU.subtract).then_inc(shifted, 1)

            def normalize(c, s):
                g, kv, n, pos, _ = group(c, s)
                dve.wait_ge(exps_done, c * GROUPS + s + 1)
                settle(nc.vector.tensor_tensor(den[:, kv, :], den[:, kv, :], esink[:, kv, :], ALU.add))
                settle(nc.vector.reciprocal(mx[:, kv, :], den[:, kv, :]))
                for h in range(4):
                    v = sm[kv][:, 2 * h * P:(2 * h + len(pos)) * P]
                    last = nc.vector.tensor_scalar(v, v, mx[:, kv, h:h + 1], None, ALU.mult)
                last.then_inc(probs_ready, 1)

            def turn_lo(c, s, w):
                dve.wait_ge(turned_hi, turns_before(c, s) + w + 1)
                nc.vector.tensor_tensor(g_lo[:, M0 + w, :], bank[:, TRANS, :], g_hi[:, M0 + w, :].bitcast(F32),
                                        ALU.subtract).then_inc(turned_ready, 1)

            def weigh_lo(c, s):
                if s % 2:
                    g, kv, n, _, _ = group(c, s)
                    dve.wait_ge(o_hi, (c * GROUPS + s) // 2 + 1)
                    at = (slice(None), slice(Q0 + 4 * g, Q0 + 4 * g + 4), slice(n * P, (n + 1) * P))
                    nc.vector.tensor_tensor(g_lo[at], bank[:, STAT, :].rearrange("p (h q) -> p h q", h=4),
                                            g_hi[at].bitcast(F32), ALU.subtract).then_inc(o_ready, 1)

            def conv_c(c, m, n, p):
                scaled2(n + (3 * m + 1) * DS, p + 3 * m)

            def scaled2(n, p):
                dve.wait_ge(multiplied, n)
                nc.vector.tensor_tensor(t_(0), bank[:, p % 4, :], rs2[:, :], ALU.mult).then_inc(panel_read, 1)

            def conv_v(c, m, n, p):
                if c:
                    nc.vector.tensor_copy(z[:, 0:2], carry[:, m, :])
                else:
                    nc.vector.memset(z[:, 0:2], 0.0)
                dve.wait_ge(multiplied, n + (3 * m + 2) * DS)
                dve.wait_ge(panel_read, p + 3 * m + 1)
                nc.vector.tensor_tensor(z[:, 2:T + 2], bank[:, (p + 3 * m + 1) % 4, :], t_(0), ALU.mult)\
                  .then_inc(panel_read, 1)
                dve.wait_ge(panel_read, p + 3 * m + 2)
                taps = [vec[:, V_CONV + 3 * m + k:V_CONV + 3 * m + k + 1] for k in range(3)]
                nc.vector.tensor_copy(carry[:, m, :], z[:, T:T + 2])
                settle(nc.vector.tensor_scalar(t_(1), z[:, 0:T], taps[0], None, ALU.mult))
                for k in (1, 2):
                    settle(nc.vector.scalar_tensor_tensor(out=t_(1), in0=z[:, k:k + T], scalar=taps[k],
                                                          in1=t_(1), op0=ALU.mult, op1=ALU.add))

            def conv_b(c, m, n, p):
                scaled(n + (3 * m + 3) * DS, 0, p + 3 * m + 2, t_(2))
                dve.wait_ge(panel_read, p + 3 * m + 3)
                nc.vector.tensor_tensor(t_(2), t_(1), t_(2), ALU.mult).then_inc(conv_sum, 1)

            def conv_lo(c, m):
                dve.wait_ge(y_hi, c * DT + m + 1)
                nc.vector.tensor_tensor(g_lo[:, Y0 + m, :], t_(2), g_hi[:, Y0 + m, :].bitcast(F32),
                                        ALU.subtract).then_inc(y_ready, 1)

            def attention_tail(c, s, part):
                if s < 0:
                    return
                nb = len(group(c, s)[3])
                if part == 0 and nb == 2:
                    turn_lo(c, s, 0)
                if part == 1:
                    turn_lo(c, s, nb - 1)
                if part == 2:
                    weigh_lo(c, s)

            def mixer(c):
                n, p = slab0(c, "kv"), panel0(c, "kv")
                dve.wait_ge(stat_done, 4 * c + 2)
                rsqrt(5 * c + 1, rs[:, :], sh.D)
                settle(nc.vector.tensor_tensor(rs2[:, :], rs[:, :], rs[:, :], ALU.mult))
                scaled(n + DS, 0, p, t_(0))
                scaled(n + 2 * DS, 0, p + 1, t_(1))
                at = (c * BLK + 1) % KVR
                nq, pq = slab0(c, "q"), panel0(c, "q")

                def query_lo(t):
                    dve.wait_ge(q_hi, c * QT + t + 1)
                    nc.vector.scalar_tensor_tensor(
                        out=g_lo[:, Q0 + t, :], in0=t_(2 + t % 2), scalar=vec[:, V_QN:V_QN + 1],
                        in1=g_hi[:, Q0 + t, :].bitcast(F32), op0=ALU.mult, op1=ALU.subtract).then_inc(q_ready, 1)

                for t in range(QT):
                    if t >= 2:
                        query_lo(t - 2)
                        dve.wait_ge(q_ready, c * QT + t - 1)
                    scaled(nq + (t + 1) * DS, 0, pq + t, t_(2 + t % 2))
                    if t == 1:
                        dve.wait_ge(kv_hi, 2 * c + 1)
                        nc.vector.tensor_tensor(
                            v_lo[:, at:at + BLK, :].rearrange("p b (k d) -> p b k d", k=3)[:, :, 0::2, :],
                            bank[:, TRANS, :].rearrange("p (b k d) -> p b k d", b=BLK, k=2),
                            v_hi[:, at:at + BLK, :].rearrange("p b (k d) -> p b k d", k=3)[:, :, 0::2, :]
                            .bitcast(F32), ALU.subtract).then_inc(kv_ready, 1)
                        dve.wait_ge(stat_done, 4 * c + 3)
                        rsqrt(5 * c + 2, var, sh.hd)
                        nc.vector.tensor_tensor(t_(0), t_(0), var, ALU.mult).then_inc(k_scaled, 1)
                        dve.wait_ge(kv_hi, 2 * c + 2)
                        nc.vector.scalar_tensor_tensor(
                            out=k_lo[:, at:at + BLK, :], in0=t_(0).rearrange("p (b d) -> p b d", b=BLK),
                            scalar=vec[:, V_KN:V_KN + 1], in1=k_hi[:, at:at + BLK, :].bitcast(F32),
                            op0=ALU.mult, op1=ALU.subtract).then_inc(kv_ready, 1)
                query_lo(QT - 2)
                query_lo(QT - 1)
                dve.wait_ge(q_summed, (c + 1) * QT)
                rsqrt(5 * c + 3, rq[:, :], sh.hd, cols=2 * QT * BLK, scale=SCALE)
                n, p = slab0(c, "conv"), panel0(c, "conv")
                for m in range(DT):
                    a = 2 * m
                    attention_tail(c, a - 1, 0)
                    mask_and_max(c, a)
                    conv_c(c, m, n, p)
                    if m:
                        conv_lo(c, m - 1)
                    attention_tail(c, a - 1, 1)
                    normalize(c, a)
                    attention_tail(c, a - 1, 2)
                    conv_v(c, m, n, p)
                    attention_tail(c, a, 0)
                    mask_and_max(c, a + 1)
                    attention_tail(c, a, 1)
                    normalize(c, a + 1)
                    conv_b(c, m, n, p)
                    attention_tail(c, a, 2)
                conv_lo(c, DT - 1)
                n, p = slab0(c, "merge"), panel0(c, "merge")

                def merged_lo(m0, off):
                    dve.wait_ge(merged_hi, c * DT + m0 + 1 + off)
                    nc.vector.tensor_tensor(g_lo[:, off + (M0 + m0), :], t_(2),
                                            g_hi[:, off + (M0 + m0), :].bitcast(F32), ALU.subtract)\
                      .then_inc(merged_ready, 1)

                def merge(m0, off):
                    sl = off * (4 * DS)
                    if m0 == 0:
                        attention_tail(c, GROUPS - 1, 0)
                    scaled(n + (4 * m0 + 1) * DS, sl, p + 4 * m0, t_(0))
                    if m0 == 0:
                        attention_tail(c, GROUPS - 1, 1)
                        attention_tail(c, GROUPS - 1, 2)
                    else:
                        merged_lo(m0 - 1, off)
                    scaled(n + (4 * m0 + 2) * DS, sl, p + 4 * m0 + 1, t_(1))
                    wait(dve, merged_ready, c * DT + m0 + off)
                    for j in range(2):
                        dve.wait_ge(gate_done, 2 * (c * DT + m0) + j + 1 + off * 2)
                        dve.wait_ge(multiplied, n + (4 * m0 + 3 + j) * DS + sl)
                        nc.vector.tensor_tensor(t_(2 + j), bank[:, (p + 2 + j) % 4, :], t_(j), ALU.mult)\
                          .then_inc(panel_read, 1)
                    dve.wait_ge(panel_read, p + 4 * m0 + 4 + off * 4)
                    nc.vector.tensor_tensor(t_(2), t_(2), t_(3), ALU.add).then_inc(merged, 1)

                merge(0, 0)
                with dve.Fori(0, DT - 1) as i:
                    merge(1, i)
                merged_lo(DT - 1, 0)
                residual(c, "out", DS, 2, 1.0)

            nc.vector.memset(v_hi[:, :, sh.hd:2 * sh.hd].bitcast(F32), 0.0)
            nc.vector.memset(v_lo[:, :, sh.hd:2 * sh.hd].bitcast(F32), 0.0)
            dve.wait_ge(const_landed, 32)
            for m in range(DT):
                prep(0, 0, m, 0, m % 4)
            for c in range(CH):
                ffn(c, 0)
                mixer(c)
                ffn(c, 1)


def kernel(**inputs):
    import numpy as np
    import concourse.bacc as bacc
    from concourse.bass_utils import run_bass_kernel_spmd

    a = {k: np.asarray(v) for k, v in inputs.items()}
    x = a["x"][0]
    S, D = x.shape
    F = a["ffn1_w_gate"].shape[-1]
    hd, heads, kvh = a["q_norm"].shape[-1], a["sinks"].shape[-1], 2
    sh = Shapes(D, S, F, heads, kvh, hd)

    def tiles(w, ns):
        k, m = w.shape
        t = np.zeros((ns * SLAB, P, m), w.dtype)
        t[:k // P] = w.reshape(k // P, P, m)
        return t.reshape(ns, SLAB, P, m // P, P).transpose(3, 0, 2, 1, 4).reshape(m // P, ns, P, SLAB * P)

    def mixed(*ws):
        return np.stack(ws, axis=1).reshape(-1, P, SLAB * P)

    order = np.concatenate([np.arange(h * hd, (h + 1) * hd) for t in range(heads // 2)
                            for h in (t, heads // 2 + t)])
    w_in = a["w_in"][0]
    gb, gc, vc = (w_in[:, i * D:(i + 1) * D] for i in range(3))
    q0 = 3 * D
    wq = w_in[:, q0:q0 + heads * hd][:, order]
    wkv = w_in[:, q0 + heads * hd:]
    wg = a["w_branch_gate"][0]
    stream = []
    for f in ("ffn1", "mix", "ffn2"):
        if f == "mix":
            stream += [tiles(wkv, sh.DS).reshape(-1, P, SLAB * P), tiles(wq, sh.DS).reshape(-1, P, SLAB * P),
                       mixed(tiles(gc, sh.DS), tiles(vc, sh.DS), tiles(gb, sh.DS)),
                       mixed(tiles(wg[:, :D], sh.DS), tiles(wg[:, D:], sh.DS), tiles(a["w_conv_out"][0], sh.DS),
                             tiles(a["w_attn_out"][0][order], sh.DS)),
                       tiles(a["w_out"][0], sh.DS).reshape(-1, P, SLAB * P)]
        else:
            stream += [mixed(tiles(a[f + "_w_gate"][0], sh.DS), tiles(a[f + "_w_up"][0], sh.DS)),
                       tiles(a[f + "_w_down"][0], sh.FS).reshape(-1, P, SLAB * P)]
    slabs = np.concatenate(stream)

    def column(v):
        return v.reshape(-1, P).T

    vectors = np.concatenate(
        [column(a[k][0]) for k in ("ffn1_norm", "mix_norm", "ffn2_norm")]
        + [a["conv_w"][0].reshape(3, -1, P).transpose(2, 1, 0).reshape(P, -1), column(a["b_branch_gate"][0]),
           np.broadcast_to(a["sinks"][0], (P, heads)),
           np.tile(a["q_norm"][0], 2)[:, None], np.tile(a["k_norm"][0], 2)[:, None]], axis=1)

    i, j = np.arange(P)[:, None], np.arange(P)[None, :]
    before, now = np.where(j > i, 0.0, NEG), np.where(j <= i, 0.0, NEG)
    half = np.arange(P) // hd
    consts = np.concatenate([before, now, before, np.eye(P), np.ones((P, P)),
                             half[:, None] == half[None, :], half[:, None] == np.arange(2)[None, :]],
                            axis=1).astype(np.float32)
    xt = x.reshape(sh.CH, T, sh.DT, P).transpose(0, 2, 3, 1)

    arrays = {"x_t": xt, "w_slabs": slabs, "shape_consts": consts, "vectors": vectors}
    arrays = {k: np.ascontiguousarray(v) for k, v in arrays.items()}
    nc = bacc.Bacc("TRN2", target_bir_lowering=False, num_devices=1)
    aps = [nc.dram_tensor(k, v.shape, mybir.dt.from_np(v.dtype), kind="ExternalInput").ap()
           for k, v in arrays.items()]
    out = nc.dram_tensor("out_t", xt.shape, F32, kind="ExternalOutput").ap()
    block_program(nc, sh, *aps, out)
    r = run_bass_kernel_spmd(nc, [arrays], core_ids=[0])
    got = r.results[0]["out_t"]
    return got.transpose(0, 3, 1, 2).reshape(1, S, D)
```

```python
from contextlib import ExitStack

import concourse.bass as bass
from concourse import mybir

F32 = mybir.dt.float32
F32R = mybir.dt.float32r
ALU = mybir.AluOpType
ACT = mybir.ActivationFunctionType
AX_X = mybir.AxisListType.X

P = 128
T = 512
SLAB = 4
RING = 4
EPS = 1e-6
NEG = -1e30
C_MASK, C_IDENT, C_ONES, C_HALVES, C_SEL, C_END = 0, 384, 512, 640, 768, 770


class Shapes:

    def __init__(s, D, S, F, heads, kv_heads, hd):
        s.D, s.S, s.F, s.hd = D, S, F, hd
        s.DT, s.FT, s.CH = D // P, F // P, S // T
        s.QT = heads * hd // P
        s.BLK = T // P
        s.DS = s.DT // SLAB
        s.FS = -(-s.FT // SLAB)
        assert kv_heads == 2 and 2 * hd == P and s.DT == s.QT == 8 and s.FT % 2 == 0
        up, down = (s.FT * 2 * s.DS, s.FT * 2), (s.DT * s.FS, s.DT)
        sizes = [("up0", up), ("down0", down), ("kv", (2 * s.DS, 2)), ("q", (s.QT * s.DS, s.QT)),
                 ("conv", (3 * s.DT * s.DS, 3 * s.DT)), ("merge", (4 * s.DT * s.DS, 4 * s.DT)),
                 ("out", (s.DT * s.DS, s.DT)), ("up1", up), ("down1", down)]
        s.slab_at, s.panel_at, s.slabs, s.panels = {}, {}, 0, 0
        for name, (ns, np_) in sizes:
            s.slab_at[name], s.panel_at[name] = s.slabs, s.panels
            s.slabs, s.panels = s.slabs + ns, s.panels + np_
        assert s.slabs % RING == 0
        assert all(v % RING == 0 for v in s.slab_at.values())


def block_program(nc, sh, x, slabs, consts, vectors, out):
    DT, FT, QT, DS, FS, CH, BLK = sh.DT, sh.FT, sh.QT, sh.DS, sh.FS, sh.CH, sh.BLK
    W = SLAB * P
    GROUPS = 4 * BLK
    LATE = 2
    KVR = BLK + 1
    V_NORM, V_CONV, V_BIAS, V_SINK, V_QN, V_KN = 0, 3 * DT, 6 * DT, 8 * DT, 8 * DT + 16, 8 * DT + 17
    SCALE = float(sh.hd) ** -0.5

    with ExitStack() as ctx:
        def sb(name, shape, dt=F32):
            return ctx.enter_context(nc.sbuf_tensor(name, shape, dt))

        def sem(name):
            return ctx.enter_context(nc.semaphore(name))

        bank = ctx.enter_context(nc.psum_tensor("bank", [P, 8, T], F32))
        SCORES, TRANS, STAT = 4, 6, 7

        raw = sb("raw", [P, RING, W])
        w_hi = sb("w_hi", [P, RING, W], F32R)
        w_lo = sb("w_lo", [P, RING, W], F32R)
        res = sb("res", [P, DT, T])
        h_hi = sb("h_hi", [P, DT, T], F32R)
        h_lo = sb("h_lo", [P, DT, T], F32R)
        G = max(FT, 3 * DT)
        g_hi = sb("g_hi", [P, G, T], F32R)
        g_lo = sb("g_lo", [P, G, T], F32R)
        Y0, Q0, M0 = 0, DT, 2 * DT
        k_hi = sb("k_hi", [P, KVR, P], F32R)
        k_lo = sb("k_lo", [P, KVR, P], F32R)
        v_hi = sb("v_hi", [P, KVR, 3 * sh.hd], F32R)
        v_lo = sb("v_lo", [P, KVR, 3 * sh.hd], F32R)
        tmp = sb("tmp", [P, 4 * T + 8])
        sq = sb("sq", [P, 2, T])
        nt = sb("nt", [P, 3, T])
        rs = sb("rs", [P, T])
        rs2 = sb("rs2", [P, T])
        cst = sb("cst", [P, C_END])
        vec = sb("vec", [P, vectors.shape[1]])
        carry = sb("carry", [P, DT, 2])
        rq = sb("rq", [P, 2 * QT * BLK])
        mx = sb("mx", [P, 2, 4])
        shift = sb("shift", [P, 2, 4])
        esink = sb("esink", [P, 2, 4])
        den = sb("den", [P, 2, 4])

        def t_(j):
            return tmp[:, j * T:(j + 1) * T]

        z = tmp[:, 3 * T:4 * T + 2]
        ssq, var, root = nt[:, 0, :], nt[:, 1, :], nt[:, 2, :]
        sm = [sq[:, :, :].rearrange("p a b -> p (a b)"),
              nt[:, 0:2, :].rearrange("p a b -> p (a b)")]
        ident, ones = cst[:, C_IDENT:C_IDENT + P], cst[:, C_ONES:C_ONES + P]
        halves, sel = cst[:, C_HALVES:C_HALVES + P], cst[:, C_SEL:C_SEL + 2]

        raw_landed = [sem(f"raw_landed{j}") for j in range(RING)]
        w_hi_ready = sem("w_hi_ready")
        w_lo_ready = sem("w_lo_ready")
        multiplied = sem("multiplied")
        panel_read = sem("panel_read")
        const_landed = sem("const_landed")
        vec_landed = sem("vec_landed")
        x_loaded = [sem(f"x_loaded{m}") for m in range(DT)]
        stored = [sem(f"stored{j}") for j in range(4)]
        prep_hi = sem("prep_hi")
        squared = sem("squared")
        ssq_added = sem("ssq_added")
        h_ready = sem("h_ready")
        stat_done = sem("stat_done")
        var_ready = sem("var_ready")
        root_ready = sem("root_ready")
        silu_done = sem("silu_done")
        product = sem("product")
        hid_hi = sem("hid_hi")
        hid_ready = sem("hid_ready")
        k_squared = sem("k_squared")
        v_turned = sem("v_turned")
        k_scaled = sem("k_scaled")
        kv_hi = sem("kv_hi")
        kv_ready = sem("kv_ready")
        q_hi = sem("q_hi")
        q_ready = sem("q_ready")
        q_summed = sem("q_summed")
        rq_ready = sem("rq_ready")
        scored = sem("scored")
        scores_read = sem("scores_read")
        shifted = sem("shifted")
        exps_done = sem("exps_done")
        probs_ready = sem("probs_ready")
        turned = sem("turned")
        turned_hi = sem("turned_hi")
        turned_ready = sem("turned_ready")
        weighed = sem("weighed")
        o_hi = sem("o_hi")
        o_ready = sem("o_ready")
        conv_sum = sem("conv_sum")
        y_hi = sem("y_hi")
        y_ready = sem("y_ready")
        gate_done = sem("gate_done")
        merged = sem("merged")
        merged_hi = sem("merged_hi")
        merged_ready = sem("merged_ready")
        dve_step = sem("dve_step")

        def wait(eng, s, value):
            if not isinstance(value, int) or value > 0:
                eng.wait_ge(s, value)

        def slab0(c, phase):
            return c * sh.slabs + sh.slab_at[phase]

        def panel0(c, phase):
            return c * sh.panels + sh.panel_at[phase]

        def prep0(c, stage):
            return (3 * c + stage) * DT

        def group(c, s):
            g, n = 2 * (s % 4), s // 4
            b = c * BLK + n
            now, before = (b + 1) % KVR, b % KVR
            if b == 0:
                return g, n, [now], P
            return g, n, ([before, now] if before < now else [now, before]), (0 if before < now else P)

        def turns_before(c, s):
            return 2 * (c * GROUPS + s) - min(4, c * GROUPS + s)

        block = ctx.enter_context(nc.Block())

        @block.sync
        def _(sp):
            sp.dma_start(vec[:, :], vectors).then_inc(vec_landed, 16)
            for c in range(CH):
                first = 1 if c == 0 else 0
                if c == 0:
                    for j in range(RING):
                        sp.dma_start(raw[:, j, :], slabs[j]).then_inc(raw_landed[j], 16)
                    sp.dma_start(cst[:, :], consts).then_inc(const_landed, 16)
                with sp.Fori(first, sh.slabs // RING) as i:
                    for j in range(RING):
                        sp.wait_ge(w_lo_ready, c * sh.slabs + j + 1 - RING + i * RING)
                        sp.dma_start(raw[:, j, :], slabs[i * RING + j]).then_inc(raw_landed[j], 16)

        @block.gpsimd
        def _(pool):
            with pool.Fori(0, CH * sh.slabs // RING) as i:
                for j in range(RING):
                    pool.wait_ge(w_hi_ready, i * RING + (j + 1))
                    nc.gpsimd.tensor_tensor(w_lo[:, j, :], raw[:, j, :], w_hi[:, j, :].bitcast(F32),
                                            ALU.subtract).then_inc(w_lo_ready, 1)

        @block.tensor
        def _(pe):
            def products(n0, off, nk, b, rhs, start, stop, ready=None):
                j = n0 % RING
                wait(pe, w_hi_ready, n0 + 1 + off)
                for k in range(nk):
                    if ready:
                        pe.wait_ge(*ready(k))
                    hi, lo = rhs(k)
                    wt = w_hi[:, j, k * P:(k + 1) * P]
                    pe.matmul(bank[:, b, :], wt, hi, start=start and k == 0, stop=False)
                    pe.matmul(bank[:, b, :], wt, lo, start=False, stop=False)
                wait(pe, w_lo_ready, n0 + 1 + off)
                for k in range(nk):
                    last = pe.matmul(bank[:, b, :], w_lo[:, j, k * P:(k + 1) * P], rhs(k)[0],
                                     start=False, stop=stop and k == nk - 1)
                last.then_inc(multiplied, 1)

            def panel(n0, noff, p0, poff, tiles, hi, lo, t0=0, ready=None, gaps=None):
                wait(pe, panel_read, p0 + 1 - 4 + poff)
                ns = -(-tiles // SLAB)
                for s in range(ns):
                    nk = min(SLAB, tiles - s * SLAB)
                    products(n0 + s, noff, nk, p0 % 4,
                             lambda k, s=s: (hi[:, t0 + s * SLAB + k, :], lo[:, t0 + s * SLAB + k, :]),
                             s == 0, s == ns - 1,
                             ready and (lambda k, s=s: ready(s * SLAB + k)))
                    if gaps:
                        gaps(s)

            def sum_squares(r):
                pe.wait_ge(ssq_added, r)
                if r == DT:
                    pe.wait_ge(const_landed, 16)
                pe.matmul(bank[:, STAT, :], ones, ssq, start=True, stop=True).then_inc(stat_done, 1)

            def ffn(c, w):
                n, p = slab0(c, f"up{w}"), panel0(c, f"up{w}")
                r = prep0(c, 2 * w)

                def body(f0, off):
                    for j in range(4):
                        first = f0 == 0 and j == 0
                        panel(n + (2 * f0 + j) * DS, 2 * DS * off, p + 2 * f0 + j, 2 * off, DT, h_hi, h_lo,
                              ready=(lambda k: (h_ready, r + k + 1)) if first else None)
                        if first:
                            sum_squares(r + DT)

                body(0, 0)
                with pe.Fori(0, FT // 2 - 1) as i:
                    body(2, i * 2)
                residual(c, f"down{w}", FT, g_hi, g_lo, 0, hid_ready, (2 * c + w) * FT)

            def residual(c, phase, tiles, hi, lo, t0, sem_, base):
                ns = -(-tiles // SLAB)
                n, p = slab0(c, phase), panel0(c, phase)
                with pe.Fori(0, DT // 4) as i:
                    for j in range(4):
                        panel(n + j * ns, i * (4 * ns), p + j, i * 4, tiles, hi, lo, t0,
                              ready=(lambda k: (sem_, base + k + 1)) if j == 0 else None)

            def q_sum(c, t):
                pe.wait_ge(q_hi, c * QT + t + 1)
                if t == 0:
                    pe.wait_ge(var_ready, 5 * c + 3)
                for b in range(BLK):
                    col = b * 2 * QT + 2 * t
                    last = pe.matmul(bank[:, STAT, col:col + 2], sq[:, t % 2, b * P:(b + 1) * P], sel,
                                     start=True, stop=True)
                last.then_inc(q_summed, 1)

            def scores(c, s):
                g, n, pos, _ = group(c, s)
                a, nb = c * GROUPS + s, len(pos)
                wait(pe, scores_read, a)
                if s == 0:
                    pe.wait_ge(kv_ready, 2 * c + 2)
                    pe.wait_ge(q_ready, (c + 1) * QT)
                ks = slice(pos[0], pos[-1] + 1, pos[-1] - pos[0] or 1)
                for j in range(2):
                    for q, k, start in ((g_hi, k_hi, True), (g_hi, k_lo, False), (g_lo, k_hi, False)):
                        for kv in range(2):
                            rows = slice(sh.hd * kv, sh.hd * (kv + 1))
                            last = pe.matmul(bank[:, SCORES + kv, 2 * j * P:(2 * j + nb) * P],
                                             q[rows, Q0 + g + j, n * P:(n + 1) * P], k[rows, ks, :],
                                             start=start, stop=q is g_lo)
                last.then_inc(scored, 1)

            def turn(c, s, w):
                a, at = c * GROUPS + s, turns_before(c, s) + w
                pe.wait_ge(probs_ready, a + 1)
                if at:
                    pe.wait_ge(turned_ready, at)
                else:
                    pe.wait_ge(kv_ready, 1)
                for h in range(4):
                    last = pe.transpose(bank[:, TRANS, h * P:(h + 1) * P],
                                        sm[s % 2][:, (2 * h + w) * P:(2 * h + w + 1) * P], ident)
                last.then_inc(turned, 1)

            def weigh(c, s):
                g, n, pos, _ = group(c, s)
                pe.wait_ge(turned_ready, turns_before(c, s) + len(pos))
                wait(pe, o_ready, c * GROUPS + s)
                if s == 0:
                    pe.wait_ge(var_ready, 5 * c + 4)
                terms = [(kv, w) for kv in range(2) for w in range(len(pos))]
                for kv, w in terms:
                    cols = slice(sh.hd * kv, sh.hd * kv + P)
                    vh, vl = v_hi[:, pos[w], cols], v_lo[:, pos[w], cols]
                    ph, pl = (t[:, M0 + w, 2 * kv * P:(2 * kv + 2) * P] for t in (g_hi, g_lo))
                    o = bank[:, STAT, 0:2 * P]
                    pe.matmul(o, vh, ph, start=(kv, w) == terms[0], stop=False)
                    pe.matmul(o, vh, pl, start=False, stop=False)
                    last = pe.matmul(o, vl, ph, start=False, stop=(kv, w) == terms[-1])
                last.then_inc(weighed, 1)

            def attention_gap(c, s):
                k, part = (s - LATE) // 3, (s - LATE) % 3
                if part == 0 and 0 <= k < GROUPS:
                    scores(c, k)
                if k <= 0 or k > GROUPS:
                    return
                nb = len(group(c, k - 1)[2])
                if part == 0 and nb == 2:
                    turn(c, k - 1, 0)
                if part == 1:
                    turn(c, k - 1, nb - 1)
                if part == 2:
                    weigh(c, k - 1)

            def mixer(c):
                r = prep0(c, 1)
                n, p = slab0(c, "kv"), panel0(c, "kv")
                panel(n, 0, p, 0, DT, h_hi, h_lo, ready=lambda k: (h_ready, r + k + 1))
                sum_squares(r + DT)
                panel(n + DS, 0, p + 1, 0, DT, h_hi, h_lo)
                n, p = slab0(c, "q"), panel0(c, "q")
                for t in range(QT):
                    panel(n + t * DS, 0, p + t, 0, DT, h_hi, h_lo)
                    if t == 1:
                        wait(pe, kv_ready, 2 * c)
                        if c:
                            pe.wait_ge(turned_ready, turns_before(c, 0))
                        pe.wait_ge(panel_read, panel0(c, "kv") + 2)
                        for b in range(BLK):
                            last = pe.transpose(bank[:, TRANS, b * P:(b + 1) * P],
                                                tmp[:, T + b * P:T + (b + 1) * P], ident)
                        last.then_inc(v_turned, 1)
                        pe.wait_ge(k_squared, c + 1)
                        pe.matmul(bank[:, STAT, :], halves, root, start=True, stop=True)\
                          .then_inc(stat_done, 1)
                    if t >= 2:
                        q_sum(c, t - 2)
                n, p = slab0(c, "conv"), panel0(c, "conv")
                for j in range(3 * DT):
                    def gaps(s, j=j):
                        if j == 0:
                            q_sum(c, QT - 2 + s)
                        attention_gap(c, 2 * j + s)
                    panel(n + j * DS, 0, p + j, 0, DT, h_hi, h_lo, gaps=gaps)
                n, p = slab0(c, "merge"), panel0(c, "merge")

                def merge(m0, off, tail=False):
                    for j, (hi, lo, t0) in enumerate([(h_hi, h_lo, 0), (h_hi, h_lo, 0),
                                                      (g_hi, g_lo, Y0), (g_hi, g_lo, Q0)]):
                        if tail and j == 2:
                            pe.wait_ge(y_ready, (c + 1) * DT)
                        if tail and j == 3:
                            pe.wait_ge(o_ready, (c + 1) * GROUPS)
                        panel(n + (4 * m0 + j) * DS, off * (4 * DS), p + 4 * m0 + j, off * 4, DT, hi, lo, t0,
                              gaps=(lambda s, j=j: attention_gap(c, (3 * DT + j) * DS + s)) if tail and j < 3
                              else None)

                merge(0, 0, tail=True)
                with pe.Fori(0, DT - 1) as i:
                    merge(1, i)
                residual(c, "out", DT, g_hi, g_lo, M0, merged_ready, c * DT)

            for c in range(CH):
                ffn(c, 0)
                mixer(c)
                ffn(c, 1)

        @block.scalar
        def _(act):
            total = CH * sh.slabs

            def split(n0, off, final=False):
                j = n0 % RING
                if n0 >= total and final:
                    return
                wait(act, multiplied, n0 + 1 - RING + off)
                act.wait_ge(raw_landed[j], 16 * (n0 // RING + 1) + off * (16 // RING))
                nc.scalar.activation(w_hi[:, j, :], raw[:, j, :], ACT.Copy).then_inc(w_hi_ready, 1)

            def prep(c, stage, m0, off, j):
                r = prep0(c, stage) + m0
                wait(act, ssq_added, r - 1 + off)
                m = off + m0
                nc.scalar.activation(h_hi[:, m, :], res[:, m, :], ACT.Copy,
                                     scale=vec[:, bass.ds(V_NORM + stage * DT + m, 1)])\
                  .then_inc(prep_hi, 1)
                nc.scalar.activation(sq[:, j % 2, :], res[:, m, :], ACT.Square).then_inc(squared, 1)

            def square_root(e):
                act.wait_ge(var_ready, e + 1)
                if e % 5 == 3:
                    nc.scalar.activation(root[:, 0:2 * QT * BLK], var[:, 0:2 * QT * BLK], ACT.Sqrt)\
                      .then_inc(root_ready, 1)
                else:
                    nc.scalar.activation(root, var, ACT.Sqrt).then_inc(root_ready, 1)

            def load_x(c, m):
                act.dma_start(res[:, m, :], x[c, m]).then_inc(x_loaded[m], 16)

            def ffn(c, w):
                n, p, fb = slab0(c, f"up{w}"), panel0(c, f"up{w}"), (2 * c + w) * FT
                ahead = RING - 1

                def body(f0, off):
                    for j in range(2):
                        f = f0 + j
                        for s in range(DS):
                            split(n + 2 * f * DS + s + ahead, off * (2 * DS))
                        if f == 0:
                            square_root(5 * c + 4 * w)
                        act.wait_ge(panel_read, p + 2 * f + 1 + off * 2)
                        nc.scalar.activation(t_(j), t_(j), ACT.Silu).then_inc(silu_done, 1)
                        for s in range(DS):
                            split(n + (2 * f + 1) * DS + s + ahead, off * (2 * DS))
                        act.wait_ge(product, fb + f + 1 + off)
                        nc.scalar.activation(g_hi[:, off + f, :], t_(2 + j), ACT.Copy).then_inc(hid_hi, 1)

                body(0, 0)
                with act.Fori(0, FT // 2 - 1) as i:
                    body(2, i * 2)
                if w == 0:
                    residual(c, "down0", FS, 1)
                else:
                    output(c)

            def residual(c, phase, ns, stage):
                n, p = slab0(c, phase), panel0(c, phase)
                with act.Fori(0, DT // 4) as i:
                    for j in range(4):
                        for s in range(ns):
                            split(n + j * ns + s + RING - 1, i * (4 * ns))
                        act.wait_ge(panel_read, p + j + 1 + i * 4)
                        prep(c, stage, j, i * 4, j)

            def output(c):
                n, p = slab0(c, "down1"), panel0(c, "down1")
                more = c + 1 < CH

                for m in range(DT):
                    for s in range(FS):
                        split(n + m * FS + s + RING - 1, 0, True)
                    if more and m:
                        act.wait_ge(x_loaded[m - 1], 16 * (c + 2))
                        prep(c + 1, 0, m - 1, 0, (m - 1) % 4)
                    act.wait_ge(panel_read, p + m + 1)
                    if more:
                        load_x(c + 1, m)
                    act.dma_start(out[c, m], t_(m % 4)).then_inc(stored[m % 4], 16)
                if more:
                    act.wait_ge(x_loaded[DT - 1], 16 * (c + 2))
                    prep(c + 1, 0, DT - 1, 0, 3)

            def exps(c, s):
                b, pos = s % 2, group(c, s)[2]
                act.wait_ge(shifted, c * GROUPS + s + 1)
                for h in range(4):
                    v = sm[b][:, 2 * h * P:(2 * h + len(pos)) * P]
                    nc.scalar.activation(v, v, ACT.Exp, bias=shift[:, b, h:h + 1],
                                         accum_out=den[:, b, h:h + 1])
                nc.scalar.activation(esink[:, b, :], esink[:, b, :], ACT.Exp).then_inc(exps_done, 1)

            def turn_hi(c, s, w):
                act.wait_ge(turned, turns_before(c, s) + w + 1)
                nc.scalar.activation(g_hi[:, M0 + w, :], bank[:, TRANS, :], ACT.Copy).then_inc(turned_hi, 1)

            def weigh_hi(c, s):
                g, n = group(c, s)[:2]
                act.wait_ge(weighed, c * GROUPS + s + 1)
                nc.scalar.activation(g_hi[:, Q0 + g:Q0 + g + 2, n * P:(n + 1) * P],
                                     bank[:, STAT, 0:2 * P].rearrange("p (h q) -> p h q", h=2), ACT.Copy)\
                  .then_inc(o_hi, 1)

            def conv_hi(c, m):
                act.wait_ge(conv_sum, c * DT + m + 1)
                nc.scalar.activation(g_hi[:, Y0 + m, :], t_(2), ACT.Copy).then_inc(y_hi, 1)

            def attention_gap(c, s):
                if s % (3 * DS) == 1 and s > 1:
                    conv_hi(c, s // (3 * DS) - 1)
                k, part = (s - LATE) // 3, (s - LATE) % 3
                if k < 0 or k > GROUPS:
                    return
                nb = len(group(c, k - 1)[2]) if k else 0
                if part == 0 and nb == 2:
                    turn_hi(c, k - 1, 0)
                if part == 1 and k:
                    turn_hi(c, k - 1, nb - 1)
                if part == 1 and k < GROUPS:
                    exps(c, k)
                if part == 2 and k:
                    weigh_hi(c, k - 1)

            def mixer(c):
                n, p = slab0(c, "kv"), panel0(c, "kv")
                for s in range(DS):
                    split(n + s + RING - 1, 0)
                square_root(5 * c + 1)
                for s in range(DS):
                    split(n + DS + s + RING - 1, 0)
                at = (c * BLK + 1) % KVR
                assert at + BLK <= KVR
                n, p = slab0(c, "q"), panel0(c, "q")
                for t in range(QT):
                    for s in range(DS):
                        split(n + t * DS + s + RING - 1, 0)
                    if t == 0:
                        act.wait_ge(panel_read, p - 1)
                        nc.scalar.activation(root, t_(0), ACT.Square).then_inc(k_squared, 1)
                    act.wait_ge(panel_read, p + t + 1)
                    if t >= 2:
                        act.wait_ge(q_summed, c * QT + t - 1)
                    nc.scalar.activation(sq[:, t % 2, :], t_(2 + t % 2), ACT.Square)
                    nc.scalar.activation(g_hi[:, Q0 + t, :], t_(2 + t % 2), ACT.Copy,
                                         scale=vec[:, V_QN:V_QN + 1]).then_inc(q_hi, 1)
                    if t == 1:
                        act.wait_ge(v_turned, c + 1)
                        nc.scalar.activation(
                            v_hi[:, at:at + BLK, :].rearrange("p b (k d) -> p b k d", k=3)[:, :, 0::2, :],
                            bank[:, TRANS, :].rearrange("p (b k d) -> p b k d", b=BLK, k=2), ACT.Copy)\
                          .then_inc(kv_hi, 1)
                        square_root(5 * c + 2)
                    if t == 4:
                        act.wait_ge(k_scaled, c + 1)
                        nc.scalar.activation(k_hi[:, at:at + BLK, :],
                                             t_(0).rearrange("p (b d) -> p b d", b=BLK), ACT.Copy,
                                             scale=vec[:, V_KN:V_KN + 1]).then_inc(kv_hi, 1)
                n = slab0(c, "conv")
                for s in range(3 * DT * DS):
                    split(n + s + RING - 1, 0)
                    if s == 0:
                        square_root(5 * c + 3)
                    attention_gap(c, s)
                n, p = slab0(c, "merge"), panel0(c, "merge")

                def merge(m0, off, tail=False):
                    for j in range(4):
                        for s in range(DS):
                            split(n + (4 * m0 + j) * DS + s + RING - 1, off * (4 * DS))
                            if tail and j < 3:
                                attention_gap(c, (3 * DT + j) * DS + s)
                        if j < 2:
                            act.wait_ge(panel_read, p + 4 * m0 + j + 1 + off * 4)
                            nc.scalar.activation(t_(j), t_(j), ACT.Sigmoid,
                                                 bias=vec[:, bass.ds(V_BIAS + j * DT + m0 + off, 1)])\
                              .then_inc(gate_done, 1)
                    act.wait_ge(merged, c * DT + m0 + 1 + off)
                    nc.scalar.activation(g_hi[:, off + (M0 + m0), :], t_(2), ACT.Copy).then_inc(merged_hi, 1)

                merge(0, 0, tail=True)
                with act.Fori(0, DT - 1) as i:
                    merge(1, i)
                residual(c, "out", DS, 2)

            for m in range(DT):
                load_x(0, m)
            split(0, 0)
            act.wait_ge(vec_landed, 16)
            for m in range(DT):
                act.wait_ge(x_loaded[m], 16)
                prep(0, 0, m, 0, m % 4)
                if m < RING - 2:
                    split(m + 1, 0)
            for c in range(CH):
                ffn(c, 0)
                mixer(c)
                ffn(c, 1)
            for j in range(4):
                act.wait_ge(stored[j], 16 * CH * DT // 4)

        @block.vector
        def _(dve):
            steps = [0]

            def settle(ins):
                steps[0] += 1
                ins.then_inc(dve_step, 1)
                dve.wait_ge(dve_step, steps[0])

            def prep(c, stage, m0, off, j):
                r, m = prep0(c, stage) + m0, off + m0
                dve.wait_ge(prep_hi, r + 1 + off)
                nc.vector.scalar_tensor_tensor(
                    out=h_lo[:, m, :], in0=res[:, m, :], scalar=vec[:, bass.ds(V_NORM + stage * DT + m, 1)],
                    in1=h_hi[:, m, :].bitcast(F32), op0=ALU.mult, op1=ALU.subtract).then_inc(h_ready, 1)
                dve.wait_ge(squared, r + 1 + off)
                if m0 == 0 and isinstance(off, int):
                    nc.vector.tensor_copy(ssq, sq[:, j % 2, :]).then_inc(ssq_added, 1)
                else:
                    wait(dve, ssq_added, r + off)
                    nc.vector.tensor_tensor(ssq, ssq, sq[:, j % 2, :], ALU.add).then_inc(ssq_added, 1)

            def rsqrt(e, dst, count, cols=T, scale=None):
                v, r, y = var[:, 0:cols], root[:, 0:cols], nt[:, 0, 0:cols]
                nc.vector.tensor_scalar(v, bank[:, STAT, 0:cols], 1.0 / count, EPS, ALU.mult, ALU.add)\
                  .then_inc(var_ready, 1)
                dve.wait_ge(root_ready, e + 1)
                settle(nc.vector.reciprocal(y, r))
                settle(nc.vector.tensor_tensor(r, y, y, ALU.mult))
                settle(nc.vector.tensor_tensor(r, r, v, ALU.mult))
                settle(nc.vector.tensor_scalar(r, r, -0.5, 1.5, ALU.mult, ALU.add))
                if scale:
                    settle(nc.vector.tensor_scalar(r, r, scale, None, ALU.mult))
                settle(nc.vector.tensor_tensor(dst, y, r, ALU.mult))

            def scaled(n, noff, p0, dst, poff=0):
                dve.wait_ge(multiplied, n + noff)
                return nc.vector.tensor_tensor(dst, bank[:, p0 % 4, :], rs[:, :], ALU.mult)\
                    .then_inc(panel_read, 1)

            def hidden_lo(fb, f0, off, j):
                dve.wait_ge(hid_hi, fb + f0 + 1 + off)
                nc.vector.tensor_tensor(g_lo[:, off + f0, :], t_(2 + j), g_hi[:, off + f0, :].bitcast(F32),
                                        ALU.subtract).then_inc(hid_ready, 1)

            def ffn(c, w):
                n, p, fb = slab0(c, f"up{w}"), panel0(c, f"up{w}"), (2 * c + w) * FT
                dve.wait_ge(stat_done, 4 * c + (1 if w == 0 else 4))
                rsqrt(5 * c + 4 * w, rs[:, :], sh.D)

                def body(f0, off):
                    for j in range(2):
                        f = f0 + j
                        scaled(n + (2 * f + 1) * DS, off * (2 * DS), p + 2 * f, t_(j))
                        if f:
                            hidden_lo(fb, f - 1, off, 1 - j)
                        scaled(n + (2 * f + 2) * DS, off * (2 * DS), p + 2 * f + 1, t_(2 + j))
                        dve.wait_ge(silu_done, fb + f + 1 + off)
                        dve.wait_ge(panel_read, p + 2 * f + 2 + off * 2)
                        nc.vector.tensor_tensor(t_(2 + j), t_(j), t_(2 + j), ALU.mult).then_inc(product, 1)

                body(0, 0)
                with dve.Fori(0, FT // 2 - 1) as i:
                    body(2, i * 2)
                hidden_lo(fb, FT - 1, 0, 1)
                if w == 0:
                    residual(c, "down0", FS, 1, 0.5)
                else:
                    output(c)

            def residual(c, phase, ns, stage, factor):
                n, p = slab0(c, phase), panel0(c, phase)

                def body(m0, off, first=False):
                    for j in range(4):
                        dve.wait_ge(multiplied, n + (m0 + j + 1) * ns + off * ns)
                        m = off + (m0 + j)
                        nc.vector.scalar_tensor_tensor(out=res[:, m, :], in0=bank[:, (p + j) % 4, :],
                                                       scalar=factor, in1=res[:, m, :], op0=ALU.mult,
                                                       op1=ALU.add).then_inc(panel_read, 1)
                        if m0 + j:
                            prep(c, stage, m0 + j - 1, off, (j - 1) % 4)

                body(0, 0)
                with dve.Fori(0, DT // 4 - 1) as i:
                    body(4, i * 4)
                prep(c, stage, DT - 1, 0, 3)

            def output(c):
                n, p = slab0(c, "down1"), panel0(c, "down1")
                more = c + 1 < CH
                for m in range(DT):
                    if more and m:
                        prep(c + 1, 0, m - 1, 0, (m - 1) % 4)
                    dve.wait_ge(multiplied, n + (m + 1) * FS)
                    wait(dve, stored[m % 4], 16 * (c * DT // 4 + m // 4))
                    nc.vector.scalar_tensor_tensor(out=t_(m % 4), in0=bank[:, (p + m) % 4, :], scalar=0.5,
                                                   in1=res[:, m, :], op0=ALU.mult, op1=ALU.add)\
                      .then_inc(panel_read, 1)
                if more:
                    prep(c + 1, 0, DT - 1, 0, 3)
                    for j in range(4):
                        dve.wait_ge(stored[j], 16 * (c + 1) * DT // 4)

            def mask_and_max(c, s):
                g, n, pos, mask = group(c, s)
                b, nb = s % 2, len(pos)
                dve.wait_ge(scored, c * GROUPS + s + 1)
                for h in range(4):
                    col = n * 2 * QT + 2 * (g + h % 2) + h // 2
                    last = nc.vector.scalar_tensor_tensor(
                        out=sm[b][:, 2 * h * P:(2 * h + nb) * P],
                        in0=bank[:, SCORES + h // 2, h % 2 * 2 * P:(h % 2 * 2 + nb) * P],
                        scalar=rq[:, col:col + 1], in1=cst[:, C_MASK + mask:C_MASK + mask + nb * P],
                        op0=ALU.mult, op1=ALU.add)
                last.then_inc(scores_read, 1)
                dve.wait_ge(scores_read, c * GROUPS + s + 1)
                sink = vec[:, V_SINK:V_SINK + 2 * QT].rearrange("p (k t) -> p k t", k=2)[:, :, g:g + 2]
                m, e = (t[:, b, :].rearrange("p (k t) -> p k t", k=2) for t in (mx, esink))
                v = sm[b].rearrange("p (h k) -> p h k", h=4)[:, :, 0:nb * P]
                settle(nc.vector.tensor_reduce(mx[:, b, :], v, AX_X, ALU.max))
                settle(nc.vector.tensor_tensor(m, m, sink, ALU.max))
                nc.vector.tensor_scalar(shift[:, b, :], mx[:, b, :], -1.0, None, ALU.mult)
                nc.vector.tensor_tensor(e, sink, m, ALU.subtract).then_inc(shifted, 1)

            def normalize(c, s):
                b, nb = s % 2, len(group(c, s)[2])
                dve.wait_ge(exps_done, c * GROUPS + s + 1)
                settle(nc.vector.tensor_tensor(den[:, b, :], den[:, b, :], esink[:, b, :], ALU.add))
                settle(nc.vector.reciprocal(mx[:, b, :], den[:, b, :]))
                for h in range(4):
                    v = sm[b][:, 2 * h * P:(2 * h + nb) * P]
                    last = nc.vector.tensor_scalar(v, v, mx[:, b, h:h + 1], None, ALU.mult)
                last.then_inc(probs_ready, 1)

            def turn_lo(c, s, w):
                dve.wait_ge(turned_hi, turns_before(c, s) + w + 1)
                nc.vector.tensor_tensor(g_lo[:, M0 + w, :], bank[:, TRANS, :], g_hi[:, M0 + w, :].bitcast(F32),
                                        ALU.subtract).then_inc(turned_ready, 1)

            def weigh_lo(c, s):
                g, n = group(c, s)[:2]
                dve.wait_ge(o_hi, c * GROUPS + s + 1)
                at = (slice(None), slice(Q0 + g, Q0 + g + 2), slice(n * P, (n + 1) * P))
                nc.vector.tensor_tensor(g_lo[at], bank[:, STAT, 0:2 * P].rearrange("p (h q) -> p h q", h=2),
                                        g_hi[at].bitcast(F32), ALU.subtract).then_inc(o_ready, 1)

            def conv_c(c, m, n, p):
                dve.wait_ge(multiplied, n + (3 * m + 1) * DS)
                nc.vector.tensor_tensor(t_(0), bank[:, (p + 3 * m) % 4, :], rs2[:, :], ALU.mult)\
                  .then_inc(panel_read, 1)

            def conv_v(c, m, n, p):
                if c:
                    nc.vector.tensor_copy(z[:, 0:2], carry[:, m, :])
                else:
                    nc.vector.memset(z[:, 0:2], 0.0)
                dve.wait_ge(multiplied, n + (3 * m + 2) * DS)
                dve.wait_ge(panel_read, p + 3 * m + 1)
                nc.vector.tensor_tensor(z[:, 2:T + 2], bank[:, (p + 3 * m + 1) % 4, :], t_(0), ALU.mult)\
                  .then_inc(panel_read, 1)
                dve.wait_ge(panel_read, p + 3 * m + 2)
                nc.vector.tensor_copy(carry[:, m, :], z[:, T:T + 2])

            def conv_taps(m):
                taps = [vec[:, V_CONV + 3 * m + k:V_CONV + 3 * m + k + 1] for k in range(3)]
                settle(nc.vector.tensor_scalar(t_(1), z[:, 0:T], taps[0], None, ALU.mult))
                for k in (1, 2):
                    settle(nc.vector.scalar_tensor_tensor(out=t_(1), in0=z[:, k:k + T], scalar=taps[k],
                                                          in1=t_(1), op0=ALU.mult, op1=ALU.add))

            def conv_b(c, m, n, p):
                scaled(n + (3 * m + 3) * DS, 0, p + 3 * m + 2, t_(2))
                dve.wait_ge(panel_read, p + 3 * m + 3)
                nc.vector.tensor_tensor(t_(2), t_(1), t_(2), ALU.mult).then_inc(conv_sum, 1)

            def conv_lo(c, m):
                dve.wait_ge(y_hi, c * DT + m + 1)
                nc.vector.tensor_tensor(g_lo[:, Y0 + m, :], t_(2), g_hi[:, Y0 + m, :].bitcast(F32),
                                        ALU.subtract).then_inc(y_ready, 1)

            def attention_tail(c, s, part):
                if s < 0:
                    return
                nb = len(group(c, s)[2])
                if part == 0 and nb == 2:
                    turn_lo(c, s, 0)
                if part == 1:
                    turn_lo(c, s, nb - 1)
                if part == 2:
                    weigh_lo(c, s)

            def mixer(c):
                n, p = slab0(c, "kv"), panel0(c, "kv")
                dve.wait_ge(stat_done, 4 * c + 2)
                rsqrt(5 * c + 1, rs[:, :], sh.D)
                settle(nc.vector.tensor_tensor(rs2[:, :], rs[:, :], rs[:, :], ALU.mult))
                scaled(n + DS, 0, p, t_(0))
                scaled(n + 2 * DS, 0, p + 1, t_(1))
                at = (c * BLK + 1) % KVR
                nq, pq = slab0(c, "q"), panel0(c, "q")

                def query_lo(t):
                    dve.wait_ge(q_hi, c * QT + t + 1)
                    nc.vector.scalar_tensor_tensor(
                        out=g_lo[:, Q0 + t, :], in0=t_(2 + t % 2), scalar=vec[:, V_QN:V_QN + 1],
                        in1=g_hi[:, Q0 + t, :].bitcast(F32), op0=ALU.mult, op1=ALU.subtract).then_inc(q_ready, 1)

                for t in range(QT):
                    if t >= 2:
                        query_lo(t - 2)
                        dve.wait_ge(q_ready, c * QT + t - 1)
                    scaled(nq + (t + 1) * DS, 0, pq + t, t_(2 + t % 2))
                    if t == 1:
                        dve.wait_ge(kv_hi, 2 * c + 1)
                        nc.vector.tensor_tensor(
                            v_lo[:, at:at + BLK, :].rearrange("p b (k d) -> p b k d", k=3)[:, :, 0::2, :],
                            bank[:, TRANS, :].rearrange("p (b k d) -> p b k d", b=BLK, k=2),
                            v_hi[:, at:at + BLK, :].rearrange("p b (k d) -> p b k d", k=3)[:, :, 0::2, :]
                            .bitcast(F32), ALU.subtract).then_inc(kv_ready, 1)
                        dve.wait_ge(stat_done, 4 * c + 3)
                        rsqrt(5 * c + 2, var, sh.hd)
                        nc.vector.tensor_tensor(t_(0), t_(0), var, ALU.mult).then_inc(k_scaled, 1)
                    if t == 5:
                        dve.wait_ge(kv_hi, 2 * c + 2)
                        nc.vector.scalar_tensor_tensor(
                            out=k_lo[:, at:at + BLK, :], in0=t_(0).rearrange("p (b d) -> p b d", b=BLK),
                            scalar=vec[:, V_KN:V_KN + 1], in1=k_hi[:, at:at + BLK, :].bitcast(F32),
                            op0=ALU.mult, op1=ALU.subtract).then_inc(kv_ready, 1)
                query_lo(QT - 2)
                query_lo(QT - 1)
                dve.wait_ge(q_summed, (c + 1) * QT)
                rsqrt(5 * c + 3, rq[:, :], sh.hd, cols=2 * QT * BLK, scale=SCALE)
                n, p = slab0(c, "conv"), panel0(c, "conv")
                for m in range(DT):
                    a = 2 * m
                    conv_c(c, m, n, p)
                    if m:
                        conv_lo(c, m - 1)
                    attention_tail(c, a - 2, 2)
                    attention_tail(c, a - 1, 0)
                    mask_and_max(c, a)
                    attention_tail(c, a - 1, 1)
                    conv_v(c, m, n, p)
                    normalize(c, a)
                    attention_tail(c, a - 1, 2)
                    conv_taps(m)
                    attention_tail(c, a, 0)
                    mask_and_max(c, a + 1)
                    attention_tail(c, a, 1)
                    conv_b(c, m, n, p)
                    normalize(c, a + 1)
                n, p = slab0(c, "merge"), panel0(c, "merge")

                def merged_lo(m0, off):
                    dve.wait_ge(merged_hi, c * DT + m0 + 1 + off)
                    nc.vector.tensor_tensor(g_lo[:, off + (M0 + m0), :], t_(2),
                                            g_hi[:, off + (M0 + m0), :].bitcast(F32), ALU.subtract)\
                      .then_inc(merged_ready, 1)

                def merge(m0, off):
                    sl = off * (4 * DS)
                    scaled(n + (4 * m0 + 1) * DS, sl, p + 4 * m0, t_(0))
                    if m0 == 0:
                        conv_lo(c, DT - 1)
                        attention_tail(c, GROUPS - 2, 2)
                        attention_tail(c, GROUPS - 1, 0)
                    else:
                        merged_lo(m0 - 1, off)
                    scaled(n + (4 * m0 + 2) * DS, sl, p + 4 * m0 + 1, t_(1))
                    if m0 == 0:
                        attention_tail(c, GROUPS - 1, 1)
                        attention_tail(c, GROUPS - 1, 2)
                    wait(dve, merged_ready, c * DT + m0 + off)
                    for j in range(2):
                        dve.wait_ge(gate_done, 2 * (c * DT + m0) + j + 1 + off * 2)
                        dve.wait_ge(multiplied, n + (4 * m0 + 3 + j) * DS + sl)
                        nc.vector.tensor_tensor(t_(2 + j), bank[:, (p + 2 + j) % 4, :], t_(j), ALU.mult)\
                          .then_inc(panel_read, 1)
                    dve.wait_ge(panel_read, p + 4 * m0 + 4 + off * 4)
                    nc.vector.tensor_tensor(t_(2), t_(2), t_(3), ALU.add).then_inc(merged, 1)

                merge(0, 0)
                with dve.Fori(0, DT - 1) as i:
                    merge(1, i)
                merged_lo(DT - 1, 0)
                residual(c, "out", DS, 2, 1.0)

            nc.vector.memset(v_hi[:, :, sh.hd:2 * sh.hd].bitcast(F32), 0.0)
            nc.vector.memset(v_lo[:, :, sh.hd:2 * sh.hd].bitcast(F32), 0.0)
            dve.wait_ge(vec_landed, 16)
            for m in range(DT):
                prep(0, 0, m, 0, m % 4)
            for c in range(CH):
                ffn(c, 0)
                mixer(c)
                ffn(c, 1)


def kernel(**inputs):
    import numpy as np
    import concourse.bacc as bacc
    from concourse.bass_utils import run_bass_kernel_spmd

    a = {k: np.asarray(v) for k, v in inputs.items()}
    x = a["x"][0]
    S, D = x.shape
    F = a["ffn1_w_gate"].shape[-1]
    hd, heads, kvh = a["q_norm"].shape[-1], a["sinks"].shape[-1], 2
    sh = Shapes(D, S, F, heads, kvh, hd)

    def tiles(w, ns):
        k, m = w.shape
        t = np.zeros((ns * SLAB, P, m), w.dtype)
        t[:k // P] = w.reshape(k // P, P, m)
        return t.reshape(ns, SLAB, P, m // P, P).transpose(3, 0, 2, 1, 4).reshape(m // P, ns, P, SLAB * P)

    def mixed(*ws):
        return np.stack(ws, axis=1).reshape(-1, P, SLAB * P)

    order = np.concatenate([np.arange(h * hd, (h + 1) * hd) for t in range(heads // 2)
                            for h in (t, heads // 2 + t)])
    w_in = a["w_in"][0]
    gb, gc, vc = (w_in[:, i * D:(i + 1) * D] for i in range(3))
    q0 = 3 * D
    wq = w_in[:, q0:q0 + heads * hd][:, order]
    wkv = w_in[:, q0 + heads * hd:]
    wg = a["w_branch_gate"][0]
    stream = []
    for f in ("ffn1", "mix", "ffn2"):
        if f == "mix":
            stream += [tiles(wkv, sh.DS).reshape(-1, P, SLAB * P), tiles(wq, sh.DS).reshape(-1, P, SLAB * P),
                       mixed(tiles(gc, sh.DS), tiles(vc, sh.DS), tiles(gb, sh.DS)),
                       mixed(tiles(wg[:, :D], sh.DS), tiles(wg[:, D:], sh.DS), tiles(a["w_conv_out"][0], sh.DS),
                             tiles(a["w_attn_out"][0][order], sh.DS)),
                       tiles(a["w_out"][0], sh.DS).reshape(-1, P, SLAB * P)]
        else:
            stream += [mixed(tiles(a[f + "_w_gate"][0], sh.DS), tiles(a[f + "_w_up"][0], sh.DS)),
                       tiles(a[f + "_w_down"][0], sh.FS).reshape(-1, P, SLAB * P)]
    slabs = np.concatenate(stream)

    def column(v):
        return v.reshape(-1, P).T

    vectors = np.concatenate(
        [column(a[k][0]) for k in ("ffn1_norm", "mix_norm", "ffn2_norm")]
        + [a["conv_w"][0].reshape(3, -1, P).transpose(2, 1, 0).reshape(P, -1), column(a["b_branch_gate"][0]),
           np.broadcast_to(a["sinks"][0], (P, heads)),
           np.tile(a["q_norm"][0], 2)[:, None], np.tile(a["k_norm"][0], 2)[:, None]], axis=1)

    i, j = np.arange(P)[:, None], np.arange(P)[None, :]
    before, now = np.where(j > i, 0.0, NEG), np.where(j <= i, 0.0, NEG)
    half = np.arange(P) // hd
    consts = np.concatenate([before, now, before, np.eye(P), np.ones((P, P)),
                             half[:, None] == half[None, :], half[:, None] == np.arange(2)[None, :]],
                            axis=1).astype(np.float32)
    xt = x.reshape(sh.CH, T, sh.DT, P).transpose(0, 2, 3, 1)

    arrays = {"x_t": xt, "w_slabs": slabs, "shape_consts": consts, "vectors": vectors}
    arrays = {k: np.ascontiguousarray(v) for k, v in arrays.items()}
    nc = bacc.Bacc("TRN2", target_bir_lowering=False, num_devices=1)
    aps = [nc.dram_tensor(k, v.shape, mybir.dt.from_np(v.dtype), kind="ExternalInput").ap()
           for k, v in arrays.items()]
    out = nc.dram_tensor("out_t", xt.shape, F32, kind="ExternalOutput").ap()
    block_program(nc, sh, *aps, out)
    r = run_bass_kernel_spmd(nc, [arrays], core_ids=[0])
    got = r.results[0]["out_t"]
    return got.transpose(0, 3, 1, 2).reshape(1, S, D)
```

```python
from contextlib import ExitStack

import concourse.bass as bass
from concourse import mybir

F32 = mybir.dt.float32
F32R = mybir.dt.float32r
ALU = mybir.AluOpType
ACT = mybir.ActivationFunctionType
AX_X = mybir.AxisListType.X

P = 128
T = 512
SLAB = 4
RING = 4
EPS = 1e-6
NEG = -1e30
C_MASK, C_IDENT, C_ONES, C_HALVES, C_SEL, C_END = 0, 384, 512, 640, 768, 770


class Shapes:

    def __init__(s, D, S, F, heads, kv_heads, hd):
        s.D, s.S, s.F, s.hd = D, S, F, hd
        s.DT, s.FT, s.CH = D // P, F // P, S // T
        s.QT = heads * hd // P
        s.BLK = T // P
        s.DS = s.DT // SLAB
        s.FS = -(-s.FT // SLAB)
        assert kv_heads == 2 and 2 * hd == P and s.DT == s.QT == 8 and s.FT % 2 == 0
        up, down = (s.FT * 2 * s.DS, s.FT * 2), (s.DT * s.FS, s.DT)
        sizes = [("up0", up), ("down0", down), ("kv", (2 * s.DS, 2)), ("q", (s.QT * s.DS, s.QT)),
                 ("conv", (3 * s.DT * s.DS, 3 * s.DT)), ("merge", (4 * s.DT * s.DS, 4 * s.DT)),
                 ("out", (s.DT * s.DS, s.DT)), ("up1", up), ("down1", down)]
        s.slab_at, s.panel_at, s.slabs, s.panels = {}, {}, 0, 0
        for name, (ns, np_) in sizes:
            s.slab_at[name], s.panel_at[name] = s.slabs, s.panels
            s.slabs, s.panels = s.slabs + ns, s.panels + np_
        assert s.slabs % RING == 0
        assert all(v % RING == 0 for v in s.slab_at.values())


def block_program(nc, sh, x, slabs, consts, vectors, out):
    DT, FT, QT, DS, FS, CH, BLK = sh.DT, sh.FT, sh.QT, sh.DS, sh.FS, sh.CH, sh.BLK
    W = SLAB * P
    GROUPS = 4 * BLK
    LATE = 2
    KVR = BLK + 1
    V_NORM, V_CONV, V_BIAS, V_SINK, V_QN, V_KN = 0, 3 * DT, 6 * DT, 8 * DT, 8 * DT + 16, 8 * DT + 17
    SCALE = float(sh.hd) ** -0.5

    with ExitStack() as ctx:
        def sb(name, shape, dt=F32):
            return ctx.enter_context(nc.sbuf_tensor(name, shape, dt))

        def sem(name):
            return ctx.enter_context(nc.semaphore(name))

        bank = ctx.enter_context(nc.psum_tensor("bank", [P, 8, T], F32))
        SCORES, TRANS, STAT = 4, 6, 7

        raw = sb("raw", [P, RING, W])
        w_hi = sb("w_hi", [P, RING, W], F32R)
        w_lo = sb("w_lo", [P, RING, W], F32R)
        res = sb("res", [P, DT, T])
        h_hi = sb("h_hi", [P, DT, T], F32R)
        h_lo = sb("h_lo", [P, DT, T], F32R)
        G = max(FT, 3 * DT)
        g_hi = sb("g_hi", [P, G, T], F32R)
        g_lo = sb("g_lo", [P, G, T], F32R)
        Y0, Q0, M0 = 0, DT, 2 * DT
        k_hi = [sb(f"k_hi{kv}", [P, KVR, P], F32R) for kv in range(2)]
        k_lo = sb("k_lo", [P, KVR, P], F32R)
        half = [slice(0, sh.hd), slice(sh.hd, P)]
        val = sb("val", [P, KVR, 4 * sh.hd], F32R)
        tmp = sb("tmp", [P, 4 * T + 8])
        sq = sb("sq", [P, 2, T])
        nt = sb("nt", [P, 3, T])
        rs = sb("rs", [P, T])
        rs2 = sb("rs2", [P, T])
        cst = sb("cst", [P, C_END])
        sel_r = sb("sel_r", [P, 2], F32R)
        vec = sb("vec", [P, vectors.shape[1]])
        carry = sb("carry", [P, DT, 2])
        rq = sb("rq", [P, 2 * QT * BLK])
        mx = sb("mx", [P, 2, 4])
        shift = sb("shift", [P, 2, 4])
        esink = sb("esink", [P, 2, 4])
        den = sb("den", [P, 2, 4])

        def t_(j):
            return tmp[:, j * T:(j + 1) * T]

        z = tmp[:, 3 * T:4 * T + 2]
        ssq, var, root = nt[:, 0, :], nt[:, 1, :], nt[:, 2, :]
        sm = [sq[:, :, :].rearrange("p a b -> p (a b)"),
              nt[:, 0:2, :].rearrange("p a b -> p (a b)")]
        ident, ones = cst[:, C_IDENT:C_IDENT + P], cst[:, C_ONES:C_ONES + P]
        halves, sel = cst[:, C_HALVES:C_HALVES + P], cst[:, C_SEL:C_SEL + 2]

        raw_landed = [sem(f"raw_landed{j}") for j in range(RING)]
        w_hi_ready = sem("w_hi_ready")
        w_lo_ready = sem("w_lo_ready")
        multiplied = sem("multiplied")
        panel_read = sem("panel_read")
        const_landed = sem("const_landed")
        vec_landed = sem("vec_landed")
        x_first = [sem(f"x_first{j}") for j in range(3)]
        x_loaded = [sem(f"x_loaded{m}") for m in range(DT)]
        x_early = sem("x_early")
        stored = [sem(f"stored{j}") for j in range(4)]
        prep_hi = sem("prep_hi")
        squared = sem("squared")
        ssq_added = sem("ssq_added")
        h_ready = sem("h_ready")
        stat_done = sem("stat_done")
        var_ready = sem("var_ready")
        root_ready = sem("root_ready")
        silu_done = sem("silu_done")
        product = sem("product")
        hid_hi = sem("hid_hi")
        hid_ready = sem("hid_ready")
        k_squared = sem("k_squared")
        v_turned = sem("v_turned")
        k_scaled = sem("k_scaled")
        kv_hi = sem("kv_hi")
        kv_ready = sem("kv_ready")
        q_hi = sem("q_hi")
        q_squared = sem("q_squared")
        q_squares_hi = sem("q_squares_hi")
        q_squares = sem("q_squares")
        selector = sem("selector")
        q_ready = sem("q_ready")
        q_summed = sem("q_summed")
        rq_ready = sem("rq_ready")
        scored = sem("scored")
        scores_read = sem("scores_read")
        shifted = sem("shifted")
        exps_done = sem("exps_done")
        inverted = sem("inverted")
        probs_ready = sem("probs_ready")
        turned = sem("turned")
        turned_hi = sem("turned_hi")
        turned_ready = sem("turned_ready")
        weighed = sem("weighed")
        o_hi = sem("o_hi")
        o_ready = sem("o_ready")
        conv_sum = sem("conv_sum")
        y_hi = sem("y_hi")
        y_ready = sem("y_ready")
        gate_done = sem("gate_done")
        merged = sem("merged")
        merged_hi = sem("merged_hi")
        merged_ready = sem("merged_ready")
        dve_step = sem("dve_step")

        def wait(eng, s, value):
            if not isinstance(value, int) or value > 0:
                eng.wait_ge(s, value)

        def slab0(c, phase):
            return c * sh.slabs + sh.slab_at[phase]

        def panel0(c, phase):
            return c * sh.panels + sh.panel_at[phase]

        def prep0(c, stage):
            return (3 * c + stage) * DT

        def group(c, s):
            g, n = 2 * (s % 4), s // 4
            b = c * BLK + n
            now, before = (b + 1) % KVR, b % KVR
            if b == 0:
                return g, n, [now], P
            return g, n, ([before, now] if before < now else [now, before]), (0 if before < now else P)

        def turns_before(c, s):
            return 2 * (c * GROUPS + s) - min(4, c * GROUPS + s)

        def weighed_part(kv, rows):
            return bank[rows, STAT, 2 * kv * P:(2 * kv + 2) * P].rearrange("p (h q) -> p h q", h=2)

        block = ctx.enter_context(nc.Block())

        @block.sync
        def _(sp):
            sp.dma_start(vec[:, :], vectors).then_inc(vec_landed, 16)
            for c in range(CH):
                first = 1 if c == 0 else 0
                if c == 0:
                    for j in range(RING):
                        sp.dma_start(raw[:, j, :], slabs[j]).then_inc(raw_landed[j], 16)
                    sp.dma_start(cst[:, :], consts).then_inc(const_landed, 16)
                with sp.Fori(first, sh.slabs // RING) as i:
                    for j in range(RING):
                        sp.wait_ge(w_lo_ready, c * sh.slabs + j + 1 - RING + i * RING)
                        sp.dma_start(raw[:, j, :], slabs[i * RING + j]).then_inc(raw_landed[j], 16)

        @block.gpsimd
        def _(pool):
            with pool.Fori(0, CH * sh.slabs // RING) as i:
                for j in range(RING):
                    pool.wait_ge(w_hi_ready, i * RING + (j + 1))
                    nc.gpsimd.tensor_tensor(w_lo[:, j, :], raw[:, j, :], w_hi[:, j, :].bitcast(F32),
                                            ALU.subtract).then_inc(w_lo_ready, 1)

        @block.tensor
        def _(pe):
            def products(n0, off, nk, b, rhs, start, stop, ready=None):
                j = n0 % RING
                wait(pe, w_hi_ready, n0 + 1 + off)
                for k in range(nk):
                    if ready:
                        pe.wait_ge(*ready(k))
                    hi, lo = rhs(k)
                    wt = w_hi[:, j, k * P:(k + 1) * P]
                    pe.matmul(bank[:, b, :], wt, hi, start=start and k == 0, stop=False)
                    pe.matmul(bank[:, b, :], wt, lo, start=False, stop=False)
                wait(pe, w_lo_ready, n0 + 1 + off)
                for k in range(nk):
                    last = pe.matmul(bank[:, b, :], w_lo[:, j, k * P:(k + 1) * P], rhs(k)[0],
                                     start=False, stop=stop and k == nk - 1)
                last.then_inc(multiplied, 1)

            def panel(n0, noff, p0, poff, tiles, hi, lo, t0=0, ready=None, gaps=None):
                wait(pe, panel_read, p0 + 1 - 4 + poff)
                ns = -(-tiles // SLAB)
                for s in range(ns):
                    nk = min(SLAB, tiles - s * SLAB)
                    products(n0 + s, noff, nk, p0 % 4,
                             lambda k, s=s: (hi[:, t0 + s * SLAB + k, :], lo[:, t0 + s * SLAB + k, :]),
                             s == 0, s == ns - 1,
                             ready and (lambda k, s=s: ready(s * SLAB + k)))
                    if gaps:
                        gaps(s)

            def sum_squares(r):
                pe.wait_ge(ssq_added, r)
                if r == DT:
                    pe.wait_ge(const_landed, 16)
                pe.matmul(bank[:, STAT, :], ones, ssq, start=True, stop=True).then_inc(stat_done, 1)

            def ffn(c, w):
                n, p = slab0(c, f"up{w}"), panel0(c, f"up{w}")
                r = prep0(c, 2 * w)

                def body(f0, off):
                    for j in range(4):
                        first = f0 == 0 and j == 0
                        panel(n + (2 * f0 + j) * DS, 2 * DS * off, p + 2 * f0 + j, 2 * off, DT, h_hi, h_lo,
                              ready=(lambda k: (h_ready, r + k + 1)) if first else None)
                        if first:
                            sum_squares(r + DT)

                body(0, 0)
                with pe.Fori(0, FT // 2 - 1) as i:
                    body(2, i * 2)
                residual(c, f"down{w}", FT, g_hi, g_lo, 0, hid_ready, (2 * c + w) * FT)

            def residual(c, phase, tiles, hi, lo, t0, sem_, base):
                ns = -(-tiles // SLAB)
                n, p = slab0(c, phase), panel0(c, phase)
                with pe.Fori(0, DT // 4) as i:
                    for j in range(4):
                        panel(n + j * ns, i * (4 * ns), p + j, i * 4, tiles, hi, lo, t0,
                              ready=(lambda k: (sem_, base + k + 1)) if j == 0 else None)

            def q_sum(c, t):
                pe.wait_ge(q_squares, c * QT + t + 1)
                if t == 0:
                    pe.wait_ge(selector, 1)
                    pe.wait_ge(var_ready, 5 * c + 3)
                for b in range(BLK):
                    col = b * 2 * QT + 2 * t
                    for part in (g_hi, g_lo):
                        last = pe.matmul(bank[:, STAT, col:col + 2], part[:, M0 + t, b * P:(b + 1) * P],
                                         sel_r[:, :], start=part is g_hi, stop=part is g_lo)
                last.then_inc(q_summed, 1)

            def scores(c, s):
                g, n, pos, _ = group(c, s)
                a, nb = c * GROUPS + s, len(pos)
                wait(pe, scores_read, a)
                if s == 0:
                    pe.wait_ge(kv_ready, 2 * c + 2)
                    pe.wait_ge(q_ready, (c + 1) * QT)
                ks = slice(pos[0], pos[-1] + 1, pos[-1] - pos[0] or 1)
                for j in range(2):
                    for k, rows in ((k_hi, [slice(0, P)] * 2), ([k_lo] * 2, half)):
                        for kv, q in enumerate((g_hi, g_lo)):
                            last = pe.matmul(bank[:, SCORES + kv, 2 * j * P:(2 * j + nb) * P],
                                             q[rows[kv], Q0 + g + j, n * P:(n + 1) * P], k[kv][rows[kv], ks, :],
                                             start=k is k_hi, stop=k is not k_hi)
                last.then_inc(scored, 1)

            def turn(c, s, w):
                a, at = c * GROUPS + s, turns_before(c, s) + w
                pe.wait_ge(probs_ready, a + 1)
                if at:
                    pe.wait_ge(turned_ready, at)
                else:
                    pe.wait_ge(kv_ready, 1)
                for h in range(4):
                    last = pe.transpose(bank[:, TRANS, h * P:(h + 1) * P],
                                        sm[s % 2][:, (2 * h + w) * P:(2 * h + w + 1) * P], ident)
                last.then_inc(turned, 1)

            def weigh(c, s):
                g, n, pos, _ = group(c, s)
                pe.wait_ge(turned_ready, turns_before(c, s) + len(pos))
                wait(pe, o_ready, c * GROUPS + s)
                if s == 0:
                    pe.wait_ge(var_ready, 5 * c + 4)
                for kv in range(2):
                    cols = slice(2 * kv * P, (2 * kv + 2) * P)
                    for w in range(len(pos)):
                        for probs in (g_hi, g_lo):
                            last = pe.matmul(bank[:, STAT, cols], val[:, pos[w], kv * P:(kv + 1) * P],
                                             probs[:, M0 + s % 2 * 2 + w, cols], start=w == 0 and probs is g_hi,
                                             stop=w == len(pos) - 1 and probs is g_lo)
                last.then_inc(weighed, 1)

            def attention_gap(c, s):
                k, part = (s - LATE) // 3, (s - LATE) % 3
                if part == 0 and 0 <= k < GROUPS:
                    scores(c, k)
                if part == 0 and 0 <= k - 2 < GROUPS:
                    weigh(c, k - 2)
                if not 0 <= k - 1 < GROUPS:
                    return
                nb = len(group(c, k - 1)[2])
                if part == 1 and nb == 2:
                    turn(c, k - 1, 0)
                if part == 2:
                    turn(c, k - 1, nb - 1)

            def mixer(c):
                r = prep0(c, 1)
                n, p = slab0(c, "kv"), panel0(c, "kv")
                panel(n, 0, p, 0, DT, h_hi, h_lo, ready=lambda k: (h_ready, r + k + 1))
                sum_squares(r + DT)
                panel(n + DS, 0, p + 1, 0, DT, h_hi, h_lo)
                n, p = slab0(c, "q"), panel0(c, "q")
                for t in range(QT):
                    panel(n + t * DS, 0, p + t, 0, DT, h_hi, h_lo)
                    if t == 1:
                        wait(pe, kv_ready, 2 * c)
                        if c:
                            pe.wait_ge(turned_ready, turns_before(c, 0))
                        pe.wait_ge(panel_read, panel0(c, "kv") + 2)
                        for b in range(BLK):
                            last = pe.transpose(bank[:, TRANS, b * P:(b + 1) * P],
                                                tmp[:, T + b * P:T + (b + 1) * P], ident)
                        last.then_inc(v_turned, 1)
                        pe.wait_ge(k_squared, c + 1)
                        pe.matmul(bank[:, STAT, :], halves, root, start=True, stop=True)\
                          .then_inc(stat_done, 1)
                    for q in {4: (0,), 5: (1, 2), 6: (3,), 7: (4, 5)}.get(t, ()):
                        q_sum(c, q)
                n, p = slab0(c, "conv"), panel0(c, "conv")
                for j in range(3 * DT):
                    def gaps(s, j=j):
                        if j == 0:
                            q_sum(c, QT - 2 + s)
                        attention_gap(c, 2 * j + s)
                    panel(n + j * DS, 0, p + j, 0, DT, h_hi, h_lo, gaps=gaps)
                n, p = slab0(c, "merge"), panel0(c, "merge")

                def merge(m0, off, tail=False):
                    for j, (hi, lo, t0) in enumerate([(h_hi, h_lo, 0), (h_hi, h_lo, 0),
                                                      (g_hi, g_lo, Y0), (g_hi, g_lo, Q0)]):
                        if tail and j == 2:
                            pe.wait_ge(y_ready, (c + 1) * DT)
                        o_tile = (lambda k: (o_ready, (c + 1) * GROUPS - 3 + k // 2)) if tail and j == 3 else None
                        panel(n + (4 * m0 + j) * DS, off * (4 * DS), p + 4 * m0 + j, off * 4, DT, hi, lo, t0, ready=o_tile,
                              gaps=(lambda s, j=j: attention_gap(c, (3 * DT + j) * DS + s)) if tail and j < 3
                              else None)

                merge(0, 0, tail=True)
                with pe.Fori(0, DT - 1) as i:
                    merge(1, i)
                residual(c, "out", DT, g_hi, g_lo, M0, merged_ready, c * DT)

            for c in range(CH):
                ffn(c, 0)
                mixer(c)
                ffn(c, 1)

        @block.scalar
        def _(act):
            total = CH * sh.slabs

            def split(n0, off, final=False):
                j = n0 % RING
                if n0 >= total and final:
                    return
                wait(act, multiplied, n0 + 1 - RING + off)
                act.wait_ge(raw_landed[j], 16 * (n0 // RING + 1) + off * (16 // RING))
                nc.scalar.activation(w_hi[:, j, :], raw[:, j, :], ACT.Copy).then_inc(w_hi_ready, 1)

            def prep(c, stage, m0, off, j, src=None):
                r = prep0(c, stage) + m0
                wait(act, ssq_added, r - 1 + off)
                m = off + m0
                src = res[:, m, :] if src is None else src
                nc.scalar.activation(h_hi[:, m, :], src, ACT.Copy,
                                     scale=vec[:, bass.ds(V_NORM + stage * DT + m, 1)])\
                  .then_inc(prep_hi, 1)
                nc.scalar.activation(sq[:, j % 2, :], src, ACT.Square).then_inc(squared, 1)

            def square_root(e):
                act.wait_ge(var_ready, e + 1)
                if e % 5 == 3:
                    nc.scalar.activation(root[:, 0:2 * QT * BLK], var[:, 0:2 * QT * BLK], ACT.Sqrt)\
                      .then_inc(root_ready, 1)
                else:
                    nc.scalar.activation(root, var, ACT.Sqrt).then_inc(root_ready, 1)

            def load_x(c, m):
                act.dma_start(res[:, m, :], x[c, m]).then_inc(x_loaded[m], 16)

            def load_early(c):
                act.dma_start(rs2[:, :], x[c, DT - 1]).then_inc(x_early, 16)

            def ffn(c, w):
                n, p, fb = slab0(c, f"up{w}"), panel0(c, f"up{w}"), (2 * c + w) * FT
                ahead = RING - 1

                def body(f0, off):
                    for j in range(2):
                        f = f0 + j
                        for s in range(DS):
                            split(n + 2 * f * DS + s + ahead, off * (2 * DS))
                        act.wait_ge(panel_read, p + 2 * f + 1 + off * 2)
                        nc.scalar.activation(t_(j), t_(j), ACT.Silu).then_inc(silu_done, 1)
                        for s in range(DS):
                            split(n + (2 * f + 1) * DS + s + ahead, off * (2 * DS))
                        act.wait_ge(product, fb + f + 1 + off)
                        nc.scalar.activation(g_hi[:, off + f, :], t_(2 + j), ACT.Copy).then_inc(hid_hi, 1)

                def splits(f, k):
                    for s in range(DS):
                        split(n + (2 * f + k) * DS + s + ahead, 0)

                def silu(f):
                    act.wait_ge(panel_read, p + 2 * f + 1)
                    nc.scalar.activation(t_(f), t_(f), ACT.Silu).then_inc(silu_done, 1)

                def hidden_hi(f):
                    act.wait_ge(product, fb + f + 1)
                    nc.scalar.activation(g_hi[:, f, :], t_(2 + f), ACT.Copy).then_inc(hid_hi, 1)

                splits(0, 0)
                square_root(5 * c + 4 * w)
                splits(0, 1)
                splits(1, 0)
                silu(0)
                hidden_hi(0)
                splits(1, 1)
                silu(1)
                hidden_hi(1)
                with act.Fori(0, FT // 2 - 1) as i:
                    body(2, i * 2)
                if w == 0:
                    residual(c, "down0", FS, 1)
                else:
                    output(c)

            def residual(c, phase, ns, stage):
                n, p = slab0(c, phase), panel0(c, phase)
                with act.Fori(0, DT // 4) as i:
                    for j in range(4):
                        for s in range(ns):
                            split(n + j * ns + s + RING - 1, i * (4 * ns))
                        act.wait_ge(panel_read, p + j + 1 + i * 4)
                        prep(c, stage, j, i * 4, j)

            def output(c):
                n, p = slab0(c, "down1"), panel0(c, "down1")
                more = c + 1 < CH

                if more:
                    load_early(c + 1)
                for m in range(DT):
                    for s in range(FS):
                        split(n + m * FS + s + RING - 1, 0, True)
                    if more and m:
                        act.wait_ge(x_loaded[m - 1], 16 * (c + 1))
                        prep(c + 1, 0, m - 1, 0, (m - 1) % 4)
                    if more and m == DT - 1:
                        act.wait_ge(x_early, 16 * (c + 1))
                        prep(c + 1, 0, m, 0, m % 4, rs2[:, :])
                    act.wait_ge(panel_read, p + m + 1)
                    if more:
                        load_x(c + 1, m)
                    act.dma_start(out[c, m], t_(m % 4)).then_inc(stored[m % 4], 16)
            def exps(c, s):
                b, pos = s % 2, group(c, s)[2]
                act.wait_ge(shifted, c * GROUPS + s + 1)
                for h in range(4):
                    v = sm[b][:, 2 * h * P:(2 * h + len(pos)) * P]
                    nc.scalar.activation(v, v, ACT.Exp, bias=shift[:, b, h:h + 1],
                                         accum_out=den[:, b, h:h + 1])
                nc.scalar.activation(esink[:, b, :], esink[:, b, :], ACT.Exp).then_inc(exps_done, 1)

            def normalize(c, s):
                b, pos = s % 2, group(c, s)[2]
                act.wait_ge(inverted, c * GROUPS + s + 1)
                for h in range(4):
                    v = sm[b][:, 2 * h * P:(2 * h + len(pos)) * P]
                    last = nc.scalar.activation(v, v, ACT.Copy, scale=mx[:, b, h:h + 1])
                last.then_inc(probs_ready, 1)

            def turn_hi(c, s, w):
                act.wait_ge(turned, turns_before(c, s) + w + 1)
                nc.scalar.activation(g_hi[:, M0 + s % 2 * 2 + w, :], bank[:, TRANS, :],
                                     ACT.Copy).then_inc(turned_hi, 1)

            def weigh_hi(c, s):
                g, n = group(c, s)[:2]
                act.wait_ge(weighed, c * GROUPS + s + 1)
                for kv, rows in enumerate(half):
                    last = nc.scalar.activation(g_hi[rows, Q0 + g:Q0 + g + 2, n * P:(n + 1) * P],
                                                weighed_part(kv, rows), ACT.Copy)
                last.then_inc(o_hi, 1)

            def conv_hi(c, m):
                act.wait_ge(conv_sum, c * DT + m + 1)
                nc.scalar.activation(g_hi[:, Y0 + m, :], t_(2), ACT.Copy).then_inc(y_hi, 1)

            def attention_gap(c, s):
                k, part = (s - LATE) // 3, (s - LATE) % 3
                now, last = 0 <= k < GROUPS, 0 <= k - 1 < GROUPS
                if part == 0 and 0 <= k - 2 < GROUPS:
                    weigh_hi(c, k - 2)
                nb = len(group(c, k - 1)[2]) if last else 0
                if part == 1 and nb == 2:
                    turn_hi(c, k - 1, 0)
                if part == 1 and now:
                    exps(c, k)
                if part == 2 and last:
                    turn_hi(c, k - 1, nb - 1)
                if part == 2 and now:
                    normalize(c, k)
                if s % (3 * DS) == 1 and s > 1:
                    conv_hi(c, s // (3 * DS) - 1)

            def mixer(c):
                n, p = slab0(c, "kv"), panel0(c, "kv")
                for s in range(DS):
                    split(n + s + RING - 1, 0)
                square_root(5 * c + 1)
                for s in range(DS):
                    split(n + DS + s + RING - 1, 0)
                at = (c * BLK + 1) % KVR
                assert at + BLK <= KVR
                n, p = slab0(c, "q"), panel0(c, "q")

                def query(t):
                    act.wait_ge(panel_read, p + t + 1)
                    if t >= 2:
                        act.wait_ge(q_squares, c * QT + t - 1)
                    nc.scalar.activation(sq[:, t % 2, :], t_(2 + t % 2), ACT.Square).then_inc(q_squared, 1)
                    for q, rows in zip((g_hi, g_lo), half):
                        last = nc.scalar.activation(q[rows, Q0 + t, :], t_(2 + t % 2)[rows, :], ACT.Copy,
                                                    scale=vec[rows, V_QN:V_QN + 1])
                    last.then_inc(q_hi, 1)
                    act.wait_ge(q_squared, c * QT + t + 1)
                    nc.scalar.activation(g_hi[:, M0 + t, :], sq[:, t % 2, :], ACT.Copy).then_inc(q_squares_hi, 1)

                for t in range(QT):
                    for s in range(DS):
                        split(n + t * DS + s + RING - 1, 0)
                    if t == 0:
                        act.wait_ge(panel_read, p - 1)
                        nc.scalar.activation(root, t_(0), ACT.Square).then_inc(k_squared, 1)
                    else:
                        query(t - 1)
                    if t == 2:
                        act.wait_ge(v_turned, c + 1)
                        nc.scalar.activation(
                            val[:, at:at + BLK, :].rearrange("p b (k d) -> p b k d", k=4)[:, :, 0::3, :],
                            bank[:, TRANS, :].rearrange("p (b k d) -> p b k d", b=BLK, k=2), ACT.Copy)\
                          .then_inc(kv_hi, 1)
                        square_root(5 * c + 2)
                    if t == 4:
                        act.wait_ge(k_scaled, c + 1)
                        for kv, own in enumerate(half):
                            for rows in half:
                                last = nc.scalar.activation(
                                    k_hi[kv][rows, at:at + BLK, :],
                                    t_(0)[own, :].rearrange("p (b d) -> p b d", b=BLK), ACT.Copy,
                                    scale=vec[own, V_KN:V_KN + 1])
                        last.then_inc(kv_hi, 1)
                n = slab0(c, "conv")
                for s in range(3 * DT * DS):
                    split(n + s + RING - 1, 0)
                    if s == 0:
                        query(QT - 1)
                    if s == 1:
                        square_root(5 * c + 3)
                    attention_gap(c, s)
                n, p = slab0(c, "merge"), panel0(c, "merge")

                def merge(m0, off, tail=False):
                    for j in range(4):
                        for s in range(DS):
                            split(n + (4 * m0 + j) * DS + s + RING - 1, off * (4 * DS))
                            if tail and j < 3:
                                attention_gap(c, (3 * DT + j) * DS + s)
                        if j < 2:
                            act.wait_ge(panel_read, p + 4 * m0 + j + 1 + off * 4)
                            nc.scalar.activation(t_(j), t_(j), ACT.Sigmoid,
                                                 bias=vec[:, bass.ds(V_BIAS + j * DT + m0 + off, 1)])\
                              .then_inc(gate_done, 1)
                    act.wait_ge(merged, c * DT + m0 + 1 + off)
                    nc.scalar.activation(g_hi[:, off + (M0 + m0), :], t_(2), ACT.Copy).then_inc(merged_hi, 1)

                merge(0, 0, tail=True)
                with act.Fori(0, DT - 1) as i:
                    merge(1, i)
                residual(c, "out", DS, 2)

            lots = [(0, 2), (2, 5), (5, DT)]
            for j, (m, e) in enumerate(lots):
                act.dma_start(res[:, m:e, :], x[0, m:e].rearrange("t p n -> p t n")).then_inc(x_first[j], 16)
            split(0, 0)
            act.wait_ge(vec_landed, 16)
            for j, (m0, e) in enumerate(lots):
                act.wait_ge(x_first[j], 16)
                for m in range(m0, e):
                    prep(0, 0, m, 0, m % 4)
                    if m < RING - 2:
                        split(m + 1, 0)
            act.wait_ge(const_landed, 16)
            nc.scalar.activation(sel_r[:, :], sel, ACT.Copy).then_inc(selector, 1)
            for c in range(CH):
                ffn(c, 0)
                mixer(c)
                ffn(c, 1)
            for j in range(4):
                act.wait_ge(stored[j], 16 * CH * DT // 4)

        @block.vector
        def _(dve):
            steps = [0]

            def settle(ins):
                steps[0] += 1
                ins.then_inc(dve_step, 1)
                dve.wait_ge(dve_step, steps[0])

            def prep(c, stage, m0, off, j, src=None):
                r, m = prep0(c, stage) + m0, off + m0
                dve.wait_ge(prep_hi, r + 1 + off)
                nc.vector.scalar_tensor_tensor(
                    out=h_lo[:, m, :], in0=res[:, m, :] if src is None else src, scalar=vec[:, bass.ds(V_NORM + stage * DT + m, 1)],
                    in1=h_hi[:, m, :].bitcast(F32), op0=ALU.mult, op1=ALU.subtract).then_inc(h_ready, 1)
                dve.wait_ge(squared, r + 1 + off)
                if m0 == 0 and isinstance(off, int):
                    nc.vector.tensor_copy(ssq, sq[:, j % 2, :]).then_inc(ssq_added, 1)
                else:
                    wait(dve, ssq_added, r + off)
                    nc.vector.tensor_tensor(ssq, ssq, sq[:, j % 2, :], ALU.add).then_inc(ssq_added, 1)

            def rsqrt(e, dst, count, cols=T, scale=None):
                v, r, y = var[:, 0:cols], root[:, 0:cols], nt[:, 0, 0:cols]
                nc.vector.tensor_scalar(v, bank[:, STAT, 0:cols], 1.0 / count, EPS, ALU.mult, ALU.add)\
                  .then_inc(var_ready, 1)
                dve.wait_ge(root_ready, e + 1)
                settle(nc.vector.reciprocal(y, r))
                settle(nc.vector.tensor_tensor(r, y, y, ALU.mult))
                settle(nc.vector.tensor_tensor(r, r, v, ALU.mult))
                settle(nc.vector.tensor_scalar(r, r, -0.5, 1.5, ALU.mult, ALU.add))
                if scale:
                    settle(nc.vector.tensor_scalar(r, r, scale, None, ALU.mult))
                settle(nc.vector.tensor_tensor(dst, y, r, ALU.mult))

            def scaled(n, noff, p0, dst, poff=0):
                dve.wait_ge(multiplied, n + noff)
                return nc.vector.tensor_tensor(dst, bank[:, p0 % 4, :], rs[:, :], ALU.mult)\
                    .then_inc(panel_read, 1)

            def hidden_lo(fb, f0, off, j):
                dve.wait_ge(hid_hi, fb + f0 + 1 + off)
                nc.vector.tensor_tensor(g_lo[:, off + f0, :], t_(2 + j), g_hi[:, off + f0, :].bitcast(F32),
                                        ALU.subtract).then_inc(hid_ready, 1)

            def ffn(c, w):
                n, p, fb = slab0(c, f"up{w}"), panel0(c, f"up{w}"), (2 * c + w) * FT
                dve.wait_ge(stat_done, 4 * c + (1 if w == 0 else 4))
                rsqrt(5 * c + 4 * w, rs[:, :], sh.D)

                def body(f0, off):
                    for j in range(2):
                        f = f0 + j
                        scaled(n + (2 * f + 1) * DS, off * (2 * DS), p + 2 * f, t_(j))
                        if f:
                            hidden_lo(fb, f - 1, off, 1 - j)
                        scaled(n + (2 * f + 2) * DS, off * (2 * DS), p + 2 * f + 1, t_(2 + j))
                        dve.wait_ge(silu_done, fb + f + 1 + off)
                        dve.wait_ge(panel_read, p + 2 * f + 2 + off * 2)
                        nc.vector.tensor_tensor(t_(2 + j), t_(j), t_(2 + j), ALU.mult).then_inc(product, 1)

                body(0, 0)
                with dve.Fori(0, FT // 2 - 1) as i:
                    body(2, i * 2)
                hidden_lo(fb, FT - 1, 0, 1)
                if w == 0:
                    residual(c, "down0", FS, 1, 0.5)
                else:
                    output(c)

            def residual(c, phase, ns, stage, factor):
                n, p = slab0(c, phase), panel0(c, phase)
                if c and stage == 1:
                    dve.wait_ge(x_loaded[DT - 1], 16 * c)

                def body(m0, off):
                    for j in range(4):
                        dve.wait_ge(multiplied, n + (m0 + j + 1) * ns + off * ns)
                        m = off + (m0 + j)
                        nc.vector.scalar_tensor_tensor(out=res[:, m, :], in0=bank[:, (p + j) % 4, :],
                                                       scalar=factor, in1=res[:, m, :], op0=ALU.mult,
                                                       op1=ALU.add).then_inc(panel_read, 1)
                        if m0 + j:
                            prep(c, stage, m0 + j - 1, off, (j - 1) % 4)

                body(0, 0)
                with dve.Fori(0, DT // 4 - 1) as i:
                    body(4, i * 4)
                prep(c, stage, DT - 1, 0, 3)

            def output(c):
                n, p = slab0(c, "down1"), panel0(c, "down1")
                more = c + 1 < CH
                for m in range(DT):
                    if more and m:
                        prep(c + 1, 0, m - 1, 0, (m - 1) % 4)
                    if more and m == DT - 1:
                        prep(c + 1, 0, m, 0, m % 4, rs2[:, :])
                    dve.wait_ge(multiplied, n + (m + 1) * FS)
                    wait(dve, stored[m % 4], 16 * (c * DT // 4 + m // 4))
                    nc.vector.scalar_tensor_tensor(out=t_(m % 4), in0=bank[:, (p + m) % 4, :], scalar=0.5,
                                                   in1=res[:, m, :], op0=ALU.mult, op1=ALU.add)\
                      .then_inc(panel_read, 1)
                if more:
                    for j in range(4):
                        dve.wait_ge(stored[j], 16 * (c + 1) * DT // 4)

            def masked(c, s):
                g, n, pos, mask = group(c, s)
                b, nb = s % 2, len(pos)
                dve.wait_ge(scored, c * GROUPS + s + 1)
                for h in range(4):
                    col = n * 2 * QT + 2 * (g + h % 2) + h // 2
                    last = nc.vector.scalar_tensor_tensor(
                        out=sm[b][:, 2 * h * P:(2 * h + nb) * P],
                        in0=bank[:, SCORES + h // 2, h % 2 * 2 * P:(h % 2 * 2 + nb) * P],
                        scalar=rq[:, col:col + 1], in1=cst[:, C_MASK + mask:C_MASK + mask + nb * P],
                        op0=ALU.mult, op1=ALU.add)
                last.then_inc(scores_read, 1)

            def maximum(c, s):
                g, n, pos, _ = group(c, s)
                b, nb = s % 2, len(pos)
                dve.wait_ge(scores_read, c * GROUPS + s + 1)
                sink = vec[:, V_SINK:V_SINK + 2 * QT].rearrange("p (k t) -> p k t", k=2)[:, :, g:g + 2]
                m, e = (t[:, b, :].rearrange("p (k t) -> p k t", k=2) for t in (mx, esink))
                v = sm[b].rearrange("p (h k) -> p h k", h=4)[:, :, 0:nb * P]
                settle(nc.vector.tensor_reduce(mx[:, b, :], v, AX_X, ALU.max))
                settle(nc.vector.tensor_tensor(m, m, sink, ALU.max))
                nc.vector.tensor_scalar(shift[:, b, :], mx[:, b, :], -1.0, None, ALU.mult)
                nc.vector.tensor_tensor(e, sink, m, ALU.subtract).then_inc(shifted, 1)

            def inverse(c, s):
                b = s % 2
                dve.wait_ge(exps_done, c * GROUPS + s + 1)
                settle(nc.vector.tensor_tensor(den[:, b, :], den[:, b, :], esink[:, b, :], ALU.add))
                nc.vector.reciprocal(mx[:, b, :], den[:, b, :]).then_inc(inverted, 1)

            def turn_lo(c, s, w):
                dve.wait_ge(turned_hi, turns_before(c, s) + w + 1)
                at = M0 + s % 2 * 2 + w
                nc.vector.tensor_tensor(g_lo[:, at, :], bank[:, TRANS, :], g_hi[:, at, :].bitcast(F32),
                                        ALU.subtract).then_inc(turned_ready, 1)

            def weigh_lo(c, s):
                g, n = group(c, s)[:2]
                dve.wait_ge(o_hi, c * GROUPS + s + 1)
                for kv, rows in enumerate(half):
                    at = (rows, slice(Q0 + g, Q0 + g + 2), slice(n * P, (n + 1) * P))
                    last = nc.vector.tensor_tensor(g_lo[at], weighed_part(kv, rows), g_hi[at].bitcast(F32),
                                                   ALU.subtract)
                settle(last)
                for kv, rows in enumerate(half):
                    at = (rows, slice(Q0 + g, Q0 + g + 2), slice(n * P, (n + 1) * P))
                    last = nc.vector.tensor_tensor(g_lo[at], weighed_part(kv, half[1 - kv]), g_lo[at].bitcast(F32),
                                                   ALU.add)
                last.then_inc(o_ready, 1)

            def conv_c(c, m, n, p):
                dve.wait_ge(multiplied, n + (3 * m + 1) * DS)
                nc.vector.tensor_tensor(t_(0), bank[:, (p + 3 * m) % 4, :], rs2[:, :], ALU.mult)\
                  .then_inc(panel_read, 1)

            def conv_v(c, m, n, p):
                if c:
                    nc.vector.tensor_copy(z[:, 0:2], carry[:, m, :])
                else:
                    nc.vector.memset(z[:, 0:2], 0.0)
                dve.wait_ge(multiplied, n + (3 * m + 2) * DS)
                dve.wait_ge(panel_read, p + 3 * m + 1)
                nc.vector.tensor_tensor(z[:, 2:T + 2], bank[:, (p + 3 * m + 1) % 4, :], t_(0), ALU.mult)\
                  .then_inc(panel_read, 1)
                dve.wait_ge(panel_read, p + 3 * m + 2)
                nc.vector.tensor_copy(carry[:, m, :], z[:, T:T + 2])

            def conv_tap(m, k):
                tap = vec[:, V_CONV + 3 * m + k:V_CONV + 3 * m + k + 1]
                if k == 0:
                    settle(nc.vector.tensor_scalar(t_(1), z[:, 0:T], tap, None, ALU.mult))
                else:
                    settle(nc.vector.scalar_tensor_tensor(out=t_(1), in0=z[:, k:k + T], scalar=tap,
                                                          in1=t_(1), op0=ALU.mult, op1=ALU.add))

            def conv_b(c, m, n, p):
                scaled(n + (3 * m + 3) * DS, 0, p + 3 * m + 2, t_(2))
                dve.wait_ge(panel_read, p + 3 * m + 3)
                nc.vector.tensor_tensor(t_(2), t_(1), t_(2), ALU.mult).then_inc(conv_sum, 1)

            def conv_lo(c, m):
                dve.wait_ge(y_hi, c * DT + m + 1)
                nc.vector.tensor_tensor(g_lo[:, Y0 + m, :], t_(2), g_hi[:, Y0 + m, :].bitcast(F32),
                                        ALU.subtract).then_inc(y_ready, 1)

            def attention_tail(c, s, part):
                if s < 0:
                    return
                nb = len(group(c, s)[2])
                if part == 0 and nb == 2:
                    turn_lo(c, s, 0)
                if part == 1:
                    turn_lo(c, s, nb - 1)
                if part == 2:
                    weigh_lo(c, s)

            def mixer(c):
                n, p = slab0(c, "kv"), panel0(c, "kv")
                dve.wait_ge(stat_done, 4 * c + 2)
                rsqrt(5 * c + 1, rs[:, :], sh.D)
                settle(nc.vector.tensor_tensor(rs2[:, :], rs[:, :], rs[:, :], ALU.mult))
                scaled(n + DS, 0, p, t_(0))
                scaled(n + 2 * DS, 0, p + 1, t_(1))
                at = (c * BLK + 1) % KVR
                nq, pq = slab0(c, "q"), panel0(c, "q")

                def query_lo(t):
                    dve.wait_ge(q_hi, c * QT + t + 1)
                    for q, rows, other in zip((g_hi, g_lo), half, half[::-1]):
                        last = nc.vector.scalar_tensor_tensor(
                            out=q[other, Q0 + t, :], in0=t_(2 + t % 2)[rows, :], scalar=vec[rows, V_QN:V_QN + 1],
                            in1=q[rows, Q0 + t, :].bitcast(F32), op0=ALU.mult, op1=ALU.subtract)
                    last.then_inc(q_ready, 1)
                    dve.wait_ge(q_squares_hi, c * QT + t + 1)
                    nc.vector.tensor_tensor(g_lo[:, M0 + t, :], sq[:, t % 2, :],
                                            g_hi[:, M0 + t, :].bitcast(F32), ALU.subtract)\
                      .then_inc(q_squares, 1)

                for t in range(QT):
                    if t >= 2:
                        query_lo(t - 2)
                        dve.wait_ge(q_ready, c * QT + t - 1)
                    scaled(nq + (t + 1) * DS, 0, pq + t, t_(2 + t % 2))
                    if t == 1:
                        dve.wait_ge(kv_hi, 2 * c + 1)
                        nc.vector.tensor_tensor(
                            val[:, at:at + BLK, :].rearrange("p b (k d) -> p b k d", k=4)[:, :, 1:3, :],
                            bank[:, TRANS, :].rearrange("p (b k d) -> p b k d", b=BLK, k=2),
                            val[:, at:at + BLK, :].rearrange("p b (k d) -> p b k d", k=4)[:, :, 0::3, :]
                            .bitcast(F32), ALU.subtract).then_inc(kv_ready, 1)
                        dve.wait_ge(stat_done, 4 * c + 3)
                        rsqrt(5 * c + 2, var, sh.hd)
                        nc.vector.tensor_tensor(t_(0), t_(0), var, ALU.mult).then_inc(k_scaled, 1)
                    if t == 5:
                        dve.wait_ge(kv_hi, 2 * c + 2)
                        for kv, rows in enumerate(half):
                            last = nc.vector.scalar_tensor_tensor(
                                out=k_lo[rows, at:at + BLK, :],
                                in0=t_(0)[rows, :].rearrange("p (b d) -> p b d", b=BLK),
                                scalar=vec[rows, V_KN:V_KN + 1], in1=k_hi[kv][rows, at:at + BLK, :].bitcast(F32),
                                op0=ALU.mult, op1=ALU.subtract)
                        last.then_inc(kv_ready, 1)
                query_lo(QT - 2)
                query_lo(QT - 1)
                dve.wait_ge(q_summed, (c + 1) * QT)
                rsqrt(5 * c + 3, rq[:, :], sh.hd, cols=2 * QT * BLK, scale=SCALE)
                n, p = slab0(c, "conv"), panel0(c, "conv")
                conv_c(c, 0, n, p)
                for m in range(DT):
                    a = 2 * m
                    masked(c, a)
                    maximum(c, a)
                    attention_tail(c, a - 2, 2)
                    attention_tail(c, a - 1, 0)
                    conv_v(c, m, n, p)
                    conv_tap(m, 0)
                    inverse(c, a)
                    conv_tap(m, 1)
                    conv_tap(m, 2)
                    attention_tail(c, a - 1, 1)
                    masked(c, a + 1)
                    maximum(c, a + 1)
                    attention_tail(c, a - 1, 2)
                    attention_tail(c, a, 0)
                    conv_b(c, m, n, p)
                    inverse(c, a + 1)
                    if m + 1 < DT:
                        conv_c(c, m + 1, n, p)
                    attention_tail(c, a, 1)
                    conv_lo(c, m)
                n, p = slab0(c, "merge"), panel0(c, "merge")

                def merged_lo(m0, off):
                    dve.wait_ge(merged_hi, c * DT + m0 + 1 + off)
                    nc.vector.tensor_tensor(g_lo[:, off + (M0 + m0), :], t_(2),
                                            g_hi[:, off + (M0 + m0), :].bitcast(F32), ALU.subtract)\
                      .then_inc(merged_ready, 1)

                def merge(m0, off):
                    sl = off * (4 * DS)
                    scaled(n + (4 * m0 + 1) * DS, sl, p + 4 * m0, t_(0))
                    if m0 == 0:
                        attention_tail(c, GROUPS - 2, 2)
                        attention_tail(c, GROUPS - 1, 0)
                    else:
                        merged_lo(m0 - 1, off)
                    scaled(n + (4 * m0 + 2) * DS, sl, p + 4 * m0 + 1, t_(1))
                    if m0 == 0:
                        attention_tail(c, GROUPS - 1, 1)
                        attention_tail(c, GROUPS - 1, 2)
                    wait(dve, merged_ready, c * DT + m0 + off)
                    for j in range(2):
                        dve.wait_ge(gate_done, 2 * (c * DT + m0) + j + 1 + off * 2)
                        dve.wait_ge(multiplied, n + (4 * m0 + 3 + j) * DS + sl)
                        nc.vector.tensor_tensor(t_(2 + j), bank[:, (p + 2 + j) % 4, :], t_(j), ALU.mult)\
                          .then_inc(panel_read, 1)
                    dve.wait_ge(panel_read, p + 4 * m0 + 4 + off * 4)
                    nc.vector.tensor_tensor(t_(2), t_(2), t_(3), ALU.add).then_inc(merged, 1)

                merge(0, 0)
                with dve.Fori(0, DT - 1) as i:
                    merge(1, i)
                merged_lo(DT - 1, 0)
                residual(c, "out", DS, 2, 1.0)

            dve.wait_ge(vec_landed, 16)
            for m in range(DT):
                prep(0, 0, m, 0, m % 4)
            for c in range(CH):
                ffn(c, 0)
                mixer(c)
                ffn(c, 1)


def kernel(**inputs):
    import numpy as np
    import concourse.bacc as bacc
    from concourse.bass_utils import run_bass_kernel_spmd

    a = {k: np.asarray(v) for k, v in inputs.items()}
    x = a["x"][0]
    S, D = x.shape
    F = a["ffn1_w_gate"].shape[-1]
    hd, heads, kvh = a["q_norm"].shape[-1], a["sinks"].shape[-1], 2
    sh = Shapes(D, S, F, heads, kvh, hd)

    def tiles(w, ns):
        k, m = w.shape
        t = np.zeros((ns * SLAB, P, m), w.dtype)
        t[:k // P] = w.reshape(k // P, P, m)
        return t.reshape(ns, SLAB, P, m // P, P).transpose(3, 0, 2, 1, 4).reshape(m // P, ns, P, SLAB * P)

    def mixed(*ws):
        return np.stack(ws, axis=1).reshape(-1, P, SLAB * P)

    order = np.concatenate([np.arange(h * hd, (h + 1) * hd) for t in range(heads // 2)
                            for h in (t, heads // 2 + t)])
    w_in = a["w_in"][0]
    gb, gc, vc = (w_in[:, i * D:(i + 1) * D] for i in range(3))
    q0 = 3 * D
    wq = w_in[:, q0:q0 + heads * hd][:, order]
    wkv = w_in[:, q0 + heads * hd:]
    wg = a["w_branch_gate"][0]
    stream = []
    for f in ("ffn1", "mix", "ffn2"):
        if f == "mix":
            stream += [tiles(wkv, sh.DS).reshape(-1, P, SLAB * P), tiles(wq, sh.DS).reshape(-1, P, SLAB * P),
                       mixed(tiles(gc, sh.DS), tiles(vc, sh.DS), tiles(gb, sh.DS)),
                       mixed(tiles(wg[:, :D], sh.DS), tiles(wg[:, D:], sh.DS), tiles(a["w_conv_out"][0], sh.DS),
                             tiles(a["w_attn_out"][0][order], sh.DS)),
                       tiles(a["w_out"][0], sh.DS).reshape(-1, P, SLAB * P)]
        else:
            stream += [mixed(tiles(a[f + "_w_gate"][0], sh.DS), tiles(a[f + "_w_up"][0], sh.DS)),
                       tiles(a[f + "_w_down"][0], sh.FS).reshape(-1, P, SLAB * P)]
    slabs = np.concatenate(stream)

    def column(v):
        return v.reshape(-1, P).T

    vectors = np.concatenate(
        [column(a[k][0]) for k in ("ffn1_norm", "mix_norm", "ffn2_norm")]
        + [a["conv_w"][0].reshape(3, -1, P).transpose(2, 1, 0).reshape(P, -1), column(a["b_branch_gate"][0]),
           np.broadcast_to(a["sinks"][0], (P, heads)),
           np.tile(a["q_norm"][0], 2)[:, None], np.tile(a["k_norm"][0], 2)[:, None]], axis=1)

    i, j = np.arange(P)[:, None], np.arange(P)[None, :]
    before, now = np.where(j > i, 0.0, NEG), np.where(j <= i, 0.0, NEG)
    half = np.arange(P) // hd
    consts = np.concatenate([before, now, before, np.eye(P), np.ones((P, P)),
                             half[:, None] == half[None, :], half[:, None] == np.arange(2)[None, :]],
                            axis=1).astype(np.float32)
    xt = x.reshape(sh.CH, T, sh.DT, P).transpose(0, 2, 3, 1)

    arrays = {"x_t": xt, "w_slabs": slabs, "shape_consts": consts, "vectors": vectors}
    arrays = {k: np.ascontiguousarray(v) for k, v in arrays.items()}
    nc = bacc.Bacc("TRN2", target_bir_lowering=False, num_devices=1)
    aps = [nc.dram_tensor(k, v.shape, mybir.dt.from_np(v.dtype), kind="ExternalInput").ap()
           for k, v in arrays.items()]
    out = nc.dram_tensor("out_t", xt.shape, F32, kind="ExternalOutput").ap()
    block_program(nc, sh, *aps, out)
    r = run_bass_kernel_spmd(nc, [arrays], core_ids=[0])
    got = r.results[0]["out_t"]
    return got.transpose(0, 3, 1, 2).reshape(1, S, D)
```
